# Optimizing a Trainium2 kernel written in Bass

```python
import jax, jax.numpy as jnp
from jax import lax
import numpy as np

D_MODEL = 1024
BATCH = 1
SEQ = 512
DEPTH = 1

HGRN_KDIM = 128
HGRN_VDIM = 128
HGRN_HEADS = D_MODEL // HGRN_KDIM
HGRN_WIDTH = HGRN_HEADS * HGRN_KDIM
GLA_CHUNK = 64
SG_CHUNK = 128
SG_GROUP_CH = 128
SG_GROUPS = D_MODEL // SG_GROUP_CH
SG_WIDTH = SG_GROUPS * SG_GROUP_CH
IN_SPLITS = (HGRN_WIDTH, HGRN_WIDTH, HGRN_WIDTH, HGRN_WIDTH, HGRN_WIDTH,
             SG_WIDTH, SG_WIDTH, SG_WIDTH, D_MODEL, D_MODEL)
IN_WIDTH = 5 * HGRN_WIDTH + 3 * SG_WIDTH + 2 * D_MODEL
RMS_EPS = 1e-6
LN_EPS = 1e-5
LB_FLOOR = 1e-20


def _rmsnorm(x, w, eps=RMS_EPS):
    xf = x.astype(jnp.float32)
    y = xf * lax.rsqrt(jnp.mean(xf * xf, axis=-1, keepdims=True) + eps)
    return (y * w.astype(jnp.float32)).astype(x.dtype)

def _layernorm(x, w, b, eps=LN_EPS):
    xf = x.astype(jnp.float32)
    mu = jnp.mean(xf, axis=-1, keepdims=True)
    var = jnp.mean(jnp.square(xf - mu), axis=-1, keepdims=True)
    y = (xf - mu) * lax.rsqrt(var + eps)
    return (y * w.astype(jnp.float32) + b.astype(jnp.float32)).astype(x.dtype)

def _gla_chunked(q, k, v, log_f):
    b, h, s, dk = q.shape
    dv = v.shape[-1]
    n = s // GLA_CHUNK

    def to_chunks(t):
        return jnp.moveaxis(t.reshape(b, h, n, GLA_CHUNK, t.shape[-1]), 2, 0)

    qc, kc, vc = to_chunks(q), to_chunks(k), to_chunks(v)
    gc = jnp.cumsum(to_chunks(log_f), axis=-2)
    mask = jnp.tril(jnp.ones((GLA_CHUNK, GLA_CHUNK), dtype=bool))[:, :, None]

    def step(state, xs):
        qb, kb, vb, gb = xs
        diff = gb[..., :, None, :] - gb[..., None, :, :]
        decay = jnp.where(mask, jnp.exp(jnp.where(mask, diff, 0.0)), 0.0)
        attn = jnp.einsum('bhtd,bhsd,bhtsd->bhts', qb, kb, decay)
        o = jnp.einsum('bhts,bhsv->bhtv', attn, vb)
        o = o + jnp.einsum('bhtd,bhdv->bhtv', qb * jnp.exp(gb), state)
        g_last = gb[..., -1:, :]
        k_dec = kb * jnp.exp(g_last - gb)
        state = state * jnp.exp(g_last[..., 0, :])[..., None] + jnp.einsum('bhsd,bhsv->bhdv', k_dec, vb)
        return state, o

    state0 = jnp.zeros((b, h, dk, dv), jnp.float32)
    _, outs = lax.scan(step, state0, (qc, kc, vc, gc))
    return jnp.moveaxis(outs, 0, 2).reshape(b, h, s, dv)

def _hgrn2_forget(f_raw, lb):
    z = f_raw.astype(jnp.float32)
    k = (1.0 - lb) * jax.nn.sigmoid(-z)
    log_f = jnp.logaddexp(jnp.log(jnp.maximum(lb, LB_FLOOR)),
                          jnp.log1p(-lb) + jax.nn.log_sigmoid(z))
    return k, log_f

def _hgrn2_branch(q_raw, ffwd_raw, fbwd_raw, i_raw, g_raw, lb_fwd, lb_bwd, gnorm_w):
    b, s, _ = q_raw.shape

    def heads(t):
        return t.reshape(b, s, HGRN_HEADS, -1).transpose(0, 2, 1, 3).astype(jnp.float32)

    def flip(t):
        return jnp.flip(t, axis=2)

    q = heads(jax.nn.silu(q_raw)) * (HGRN_KDIM ** -0.5)
    v = heads(i_raw)
    k_f, g_f = _hgrn2_forget(ffwd_raw, lb_fwd)
    k_b, g_b = _hgrn2_forget(fbwd_raw, lb_bwd)
    o_fwd = _gla_chunked(q, heads(k_f), v, heads(g_f))
    o_bwd = flip(_gla_chunked(flip(q), flip(heads(k_b)), flip(v), flip(heads(g_b))))
    o = (o_fwd + o_bwd).transpose(0, 2, 1, 3)
    o = _rmsnorm(o, gnorm_w).reshape(b, s, HGRN_HEADS * HGRN_VDIM)
    return (o * jax.nn.silu(g_raw.astype(jnp.float32))).astype(q_raw.dtype)

def _spatial_gating_branch(u_raw, v_raw, g_raw, ln_w, ln_b, w_s, b_s):
    b, s, _ = u_raw.shape
    u = jax.nn.gelu(u_raw)
    v = _layernorm(jax.nn.gelu(v_raw), ln_w, ln_b)
    vc = v.reshape(b, s // SG_CHUNK, SG_CHUNK, SG_GROUPS, SG_GROUP_CH)
    mixed = jnp.einsum('gts,bnsgc->bntgc', w_s, vc) + b_s.T[None, None, :, :, None]
    return u * mixed.reshape(b, s, SG_WIDTH) * jax.nn.silu(g_raw)

def first_inputs(seed: int = 0) -> dict:
    key = jax.random.key(seed)
    ks = jax.random.split(key, 16)
    f32 = jnp.float32
    x = jax.random.normal(ks[0], (BATCH, SEQ, D_MODEL), f32)
    norm_w = 1.0 + 0.05 * jax.random.normal(ks[1], (DEPTH, D_MODEL), f32)
    w_in = jax.random.normal(ks[2], (DEPTH, D_MODEL, IN_WIDTH), f32) * D_MODEL ** -0.5
    lower_bounds = 0.1 * jax.random.normal(ks[3], (DEPTH, 2, HGRN_WIDTH), f32)
    gnorm_w = 1.0 + 0.05 * jax.random.normal(ks[4], (DEPTH, HGRN_VDIM), f32)
    ln_w = 1.0 + 0.05 * jax.random.normal(ks[5], (DEPTH, SG_WIDTH), f32)
    ln_b = 0.02 * jax.random.normal(ks[6], (DEPTH, SG_WIDTH), f32)
    w_s = jax.random.normal(ks[7], (DEPTH, SG_GROUPS, SG_CHUNK, SG_CHUNK), f32) * SG_CHUNK ** -0.5
    b_s = 1.0 + 0.1 * jax.random.normal(ks[8], (DEPTH, SG_GROUPS, SG_CHUNK), f32)
    w_proj_a = jax.random.normal(ks[9], (DEPTH, HGRN_WIDTH, D_MODEL), f32) * HGRN_WIDTH ** -0.5
    w_proj_b = jax.random.normal(ks[10], (DEPTH, SG_WIDTH, D_MODEL), f32) * SG_WIDTH ** -0.5
    w_out = jax.random.normal(ks[11], (DEPTH, D_MODEL, D_MODEL), f32) * D_MODEL ** -0.5
    final_norm_w = 1.0 + 0.05 * jax.random.normal(ks[12], (D_MODEL,), f32)
    return {"x": x, "norm_w": norm_w, "w_in": w_in, "lower_bounds": lower_bounds,
            "gnorm_w": gnorm_w, "ln_w": ln_w, "ln_b": ln_b, "w_s": w_s, "b_s": b_s,
            "w_proj_a": w_proj_a, "w_proj_b": w_proj_b, "w_out": w_out,
            "final_norm_w": final_norm_w}

def first_block(x, norm_w, w_in, lower_bounds, gnorm_w, ln_w, ln_b, w_s, b_s,
              w_proj_a, w_proj_b, w_out, final_norm_w):
    lb = jax.nn.softmax(lower_bounds.astype(jnp.float32), axis=0)
    lb = jnp.cumsum(lb, axis=0) - lb[0]
    split_points = []
    acc = 0
    for size in IN_SPLITS[:-1]:
        acc += size
        split_points.append(acc)
    for layer in range(DEPTH):
        h = _rmsnorm(x, norm_w[layer])
        proj = jnp.einsum('bsd,de->bse', h, w_in[layer])
        (q_raw, ffwd_raw, fbwd_raw, i_raw, ga_raw,
         u_raw, v_raw, gb_raw, ma_raw, mb_raw) = jnp.split(proj, split_points, axis=-1)
        y_a = _hgrn2_branch(q_raw, ffwd_raw, fbwd_raw, i_raw, ga_raw,
                            lb[layer, 0], lb[layer, 1], gnorm_w[layer])
        y_b = _spatial_gating_branch(u_raw, v_raw, gb_raw, ln_w[layer], ln_b[layer],
                                     w_s[layer], b_s[layer])
        merged = (jax.nn.sigmoid(ma_raw) * jnp.einsum('bsw,wd->bsd', y_a, w_proj_a[layer])
                  + jax.nn.sigmoid(mb_raw) * jnp.einsum('bsw,wd->bsd', y_b, w_proj_b[layer]))
        x = x + jnp.einsum('bsd,de->bse', merged, w_out[layer])
    return _rmsnorm(x, final_norm_w)


DEPTH_2 = 2

GRID_W = 64
CTX_LEN = 256
N_MIXERS = 2
BLK = 128
WINDOW = 128
ROPE_BASE = 10000.0
EPS = 1e-6
NEG_INF = -1e30

A_HEADS = 16
A_KV_HEADS = 4
A_GROUP = A_HEADS // A_KV_HEADS
A_HEAD_DIM = 64
A_WIDTH = A_HEADS * A_HEAD_DIM
A_KV_WIDTH = A_KV_HEADS * A_HEAD_DIM
A_IN = A_WIDTH + 2 * A_KV_WIDTH + A_WIDTH

B_HEADS = 16
B_NOPE = 64
B_ROPE = 32
B_V = 64
B_Q_RANK = 256
B_KV_RANK = 128
B_WIDTH = B_HEADS * B_V
B_IN = B_Q_RANK + B_KV_RANK + B_ROPE + B_WIDTH


def rmsnorm(x, g):
    xf = x.astype(jnp.float32)
    y = xf * lax.rsqrt(jnp.mean(xf * xf, axis=-1, keepdims=True) + EPS)
    return (y * g.astype(jnp.float32)).astype(x.dtype)

def axial_rope_tables(n_tokens, rot_dim, dtype):
    n_rows = n_tokens // GRID_W
    row = jnp.broadcast_to(jnp.arange(n_rows)[:, None], (n_rows, GRID_W)).reshape(-1)
    col = jnp.broadcast_to(jnp.arange(GRID_W)[None, :], (n_rows, GRID_W)).reshape(-1)
    nf = rot_dim // 4
    inv = ROPE_BASE ** (-jnp.arange(nf, dtype=jnp.float32) / nf)
    ar = row.astype(jnp.float32)[:, None] * inv
    ac = col.astype(jnp.float32)[:, None] * inv
    ang = jnp.concatenate([ar, ar, ac, ac], axis=-1)
    return jnp.cos(ang).astype(dtype), jnp.sin(ang).astype(dtype)

def apply_rope(x, cos, sin):
    a1, a2, b1, b2 = jnp.split(x, 4, axis=-1)
    rot = jnp.concatenate([-a2, a1, -b2, b1], axis=-1)
    shp = (x.shape[1],) + (1,) * (x.ndim - 3) + (x.shape[-1],)
    return x * cos.reshape(shp) + rot * sin.reshape(shp)

def modulate(x, g, shift, scale):
    return rmsnorm(x, g) * (1 + scale) + shift

def mixer_a(h, hc, w_in, sinks, w_o, cos, sin, ctx_out):
    bsz, S, _ = h.shape
    dt = h.dtype
    q, k, v, g = jnp.split(h @ w_in, [A_WIDTH, A_WIDTH + A_KV_WIDTH, A_WIDTH + 2 * A_KV_WIDTH], axis=-1)
    q = apply_rope(q.reshape(bsz, S, A_KV_HEADS, A_GROUP, A_HEAD_DIM), cos, sin)
    k = apply_rope(k.reshape(bsz, S, A_KV_HEADS, A_HEAD_DIM), cos, sin)
    v = v.reshape(bsz, S, A_KV_HEADS, A_HEAD_DIM)
    kvc = hc @ w_in[:, A_WIDTH:A_WIDTH + 2 * A_KV_WIDTH]
    kc, vc = jnp.split(kvc.reshape(bsz, -1, 2 * A_KV_HEADS, A_HEAD_DIM), 2, axis=2)
    sink_logit = sinks.astype(jnp.float32).reshape(A_KV_HEADS, A_GROUP)
    scale = A_HEAD_DIM ** -0.5
    kp = jnp.pad(k, ((0, 0), (BLK, BLK), (0, 0), (0, 0)))
    vp = jnp.pad(v, ((0, 0), (BLK, BLK), (0, 0), (0, 0)))

    def block(i):
        qs = lax.dynamic_slice_in_dim(q, i * BLK, BLK, axis=1)
        ks = lax.dynamic_slice_in_dim(kp, i * BLK, 3 * BLK, axis=1)
        vs = lax.dynamic_slice_in_dim(vp, i * BLK, 3 * BLK, axis=1)
        q_pos = i * BLK + jnp.arange(BLK)
        k_pos = (i - 1) * BLK + jnp.arange(3 * BLK)
        valid = (jnp.abs(q_pos[:, None] - k_pos[None, :]) <= WINDOW) & (k_pos >= 0)[None, :] & (k_pos < S)[None, :]
        s_loc = jnp.einsum('bqhgd,bkhd->bhgqk', qs, ks).astype(jnp.float32) * scale
        s_loc = jnp.where(valid, s_loc, NEG_INF)
        s_ctx = jnp.einsum('bqhgd,bkhd->bhgqk', qs, kc).astype(jnp.float32) * scale
        sink = jnp.broadcast_to(sink_logit[None, :, :, None, None], s_loc.shape[:-1] + (1,))
        p = jax.nn.softmax(jnp.concatenate([s_loc, s_ctx, sink], axis=-1), axis=-1).astype(dt)
        n_loc = 3 * BLK
        return (jnp.einsum('bhgqk,bkhd->bqhgd', p[..., :n_loc], vs)
                + jnp.einsum('bhgqk,bkhd->bqhgd', p[..., n_loc:-1], vc))

    o = lax.map(block, jnp.arange(S // BLK))
    o = jnp.moveaxis(o, 0, 1).reshape(bsz, S, A_WIDTH)
    y = (o * jax.nn.silu(g)) @ w_o
    if not ctx_out:
        return y, None
    C = hc.shape[1]
    qc = (hc @ w_in[:, :A_WIDTH]).reshape(bsz, C, A_KV_HEADS, A_GROUP, A_HEAD_DIM)
    gc = hc @ w_in[:, A_WIDTH + 2 * A_KV_WIDTH:]
    s = jnp.einsum('bqhgd,bkhd->bhgqk', qc, kc).astype(jnp.float32) * scale
    sink = jnp.broadcast_to(sink_logit[None, :, :, None, None], s.shape[:-1] + (1,))
    p = jax.nn.softmax(jnp.concatenate([s, sink], axis=-1), axis=-1)[..., :-1].astype(dt)
    oc = jnp.einsum('bhgqk,bkhd->bqhgd', p, vc).reshape(bsz, C, A_WIDTH)
    yc = (oc * jax.nn.silu(gc)) @ w_o
    return y, yc

def mixer_b(h, hc, w_in, q_norm_g, w_uq, kv_norm_g, w_ukv, w_o, cos, sin, ctx_out):
    bsz, S, _ = h.shape
    C = hc.shape[1]
    dt = h.dtype
    splits = [B_Q_RANK, B_Q_RANK + B_KV_RANK, B_Q_RANK + B_KV_RANK + B_ROPE]
    cq, ckv, kr, g = jnp.split(h @ w_in, splits, axis=-1)
    q = (rmsnorm(cq, q_norm_g) @ w_uq).reshape(bsz, S, B_HEADS, B_NOPE + B_ROPE)
    qn, qr = q[..., :B_NOPE], apply_rope(q[..., B_NOPE:], cos, sin)
    kv = (rmsnorm(ckv, kv_norm_g) @ w_ukv).reshape(bsz, S, B_HEADS, B_NOPE + B_V)
    kn, v = kv[..., :B_NOPE], kv[..., B_NOPE:]
    kr = apply_rope(kr, cos, sin)
    ckv_c, kr_c = jnp.split(hc @ w_in[:, B_Q_RANK:splits[2]], [B_KV_RANK], axis=-1)
    kv_c = (rmsnorm(ckv_c, kv_norm_g) @ w_ukv).reshape(bsz, C, B_HEADS, B_NOPE + B_V)
    kn_c, v_c = kv_c[..., :B_NOPE], kv_c[..., B_NOPE:]
    kn_all = jnp.concatenate([kn_c, kn], axis=1)
    kr_all = jnp.concatenate([kr_c, kr], axis=1)
    v_all = jnp.concatenate([v_c, v], axis=1)
    scale = (B_NOPE + B_ROPE) ** -0.5

    def block(i):
        qn_b = lax.dynamic_slice_in_dim(qn, i * BLK, BLK, axis=1)
        qr_b = lax.dynamic_slice_in_dim(qr, i * BLK, BLK, axis=1)
        s = (jnp.einsum('bqhd,bkhd->bhqk', qn_b, kn_all)
             + jnp.einsum('bqhr,bkr->bhqk', qr_b, kr_all)).astype(jnp.float32) * scale
        p = jax.nn.softmax(s, axis=-1).astype(dt)
        return jnp.einsum('bhqk,bkhd->bqhd', p, v_all)

    o = lax.map(block, jnp.arange(S // BLK))
    o = jnp.moveaxis(o, 0, 1).reshape(bsz, S, B_WIDTH)
    y = (o * jax.nn.silu(g)) @ w_o
    if not ctx_out:
        return y, None
    qc = (rmsnorm(hc @ w_in[:, :B_Q_RANK], q_norm_g) @ w_uq).reshape(bsz, C, B_HEADS, B_NOPE + B_ROPE)
    gc = hc @ w_in[:, splits[2]:]
    s = (jnp.einsum('bqhd,bkhd->bhqk', qc[..., :B_NOPE], kn_c)
         + jnp.einsum('bqhr,bkr->bhqk', qc[..., B_NOPE:], kr_c)).astype(jnp.float32) * scale
    p = jax.nn.softmax(s, axis=-1).astype(dt)
    oc = jnp.einsum('bhqk,bkhd->bqhd', p, v_c).reshape(bsz, C, B_WIDTH)
    yc = (oc * jax.nn.silu(gc)) @ w_o
    return y, yc

def second_inputs(seed: int = 0) -> dict:
    key = jax.random.key(seed)
    ks = jax.random.split(key, 24)
    f = jnp.float32
    D = D_MODEL

    def w(k, shape, fan_in):
        return jax.random.normal(k, shape, f) * fan_in ** -0.5

    def gain(k, n):
        return 1.0 + 0.02 * jax.random.normal(k, (n,), f)

    return {
        "x": jax.random.normal(ks[0], (BATCH, SEQ, D), f),
        "c": jax.random.normal(ks[1], (BATCH, D), f),
        "ctx": jax.random.normal(ks[2], (BATCH, CTX_LEN, D), f),
        "c_ctx": jax.random.normal(ks[3], (D,), f),
        "norm_g_0": gain(ks[4], D),
        "ada_w_0": w(ks[5], (D, 3 * D), D),
        "ada_b_0": 0.02 * jax.random.normal(ks[6], (3 * D,), f),
        "a_w_in_0": w(ks[7], (D, A_IN), D),
        "a_sinks_0": 0.5 * jax.random.normal(ks[8], (A_HEADS,), f),
        "a_w_o_0": w(ks[9], (A_WIDTH, D), A_WIDTH),
        "norm_g_1": gain(ks[10], D),
        "ada_w_1": w(ks[11], (D, 3 * D), D),
        "ada_b_1": 0.02 * jax.random.normal(ks[12], (3 * D,), f),
        "b_w_in_1": w(ks[13], (D, B_IN), D),
        "b_q_norm_1": gain(ks[14], B_Q_RANK),
        "b_w_uq_1": w(ks[15], (B_Q_RANK, B_HEADS * (B_NOPE + B_ROPE)), B_Q_RANK),
        "b_kv_norm_1": gain(ks[16], B_KV_RANK),
        "b_w_ukv_1": w(ks[17], (B_KV_RANK, B_HEADS * (B_NOPE + B_V)), B_KV_RANK),
        "b_w_o_1": w(ks[18], (B_WIDTH, D), B_WIDTH),
        "final_g": gain(ks[19], D),
    }

def second_block(x, c, ctx, c_ctx, norm_g_0, ada_w_0, ada_b_0, a_w_in_0, a_sinks_0, a_w_o_0,
              norm_g_1, ada_w_1, ada_b_1, b_w_in_1, b_q_norm_1, b_w_uq_1, b_kv_norm_1,
              b_w_ukv_1, b_w_o_1, final_g):
    S = x.shape[1]
    cos_a, sin_a = axial_rope_tables(S, A_HEAD_DIM, x.dtype)
    cos_b, sin_b = axial_rope_tables(S, B_ROPE, x.dtype)
    layers = [
        (norm_g_0, ada_w_0, ada_b_0, (a_w_in_0, a_sinks_0, a_w_o_0)),
        (norm_g_1, ada_w_1, ada_b_1, (b_w_in_1, b_q_norm_1, b_w_uq_1, b_kv_norm_1, b_w_ukv_1, b_w_o_1)),
    ]
    for i in range(DEPTH_2):
        g_norm, ada_w, ada_b, mp = layers[i]
        last = i == DEPTH_2 - 1
        shift, scale, gate = jnp.split(jax.nn.silu(c) @ ada_w + ada_b, 3, axis=-1)
        shift_c, scale_c, gate_c = jnp.split(jax.nn.silu(c_ctx) @ ada_w + ada_b, 3, axis=-1)
        h = modulate(x, g_norm, shift[:, None], scale[:, None])
        hc = modulate(ctx, g_norm, shift_c, scale_c)
        if i % N_MIXERS == 0:
            y, yc = mixer_a(h, hc, *mp, cos_a, sin_a, not last)
        else:
            y, yc = mixer_b(h, hc, *mp, cos_b, sin_b, not last)
        x = x + gate[:, None] * y
        if not last:
            ctx = ctx + gate_c * yc
    return rmsnorm(x, final_g)


def setup_inputs(seed=0):
    out = dict(first_inputs(seed))
    for name, value in second_inputs(seed + 1).items():
        if name != "x":
            out[name + "_2"] = value
    return out


def reference(
    x, norm_w, w_in, lower_bounds, gnorm_w, ln_w, ln_b, w_s, b_s, w_proj_a, w_proj_b, w_out,
    final_norm_w, c_2, ctx_2, c_ctx_2, norm_g_0_2, ada_w_0_2, ada_b_0_2, a_w_in_0_2,
    a_sinks_0_2, a_w_o_0_2, norm_g_1_2, ada_w_1_2, ada_b_1_2, b_w_in_1_2, b_q_norm_1_2,
    b_w_uq_1_2, b_kv_norm_1_2, b_w_ukv_1_2, b_w_o_1_2, final_g_2,
):
    x = first_block(
        x, norm_w, w_in, lower_bounds, gnorm_w, ln_w, ln_b, w_s, b_s, w_proj_a, w_proj_b, w_out,
        final_norm_w,
    )
    return second_block(
        x, c_2, ctx_2, c_ctx_2, norm_g_0_2, ada_w_0_2, ada_b_0_2, a_w_in_0_2, a_sinks_0_2,
        a_w_o_0_2, norm_g_1_2, ada_w_1_2, ada_b_1_2, b_w_in_1_2, b_q_norm_1_2, b_w_uq_1_2,
        b_kv_norm_1_2, b_w_ukv_1_2, b_w_o_1_2, final_g_2,
    )


_drawn_inputs = setup_inputs


def setup_inputs(seed=0):
    import zlib

    import numpy as np

    out = dict(_drawn_inputs(seed))
    spreads = {}
    factors = {'gnorm_w': 3.68,
     'ln_w': 5.623,
     'ln_b': 8.0,
     'b_s': 3.073,
     'norm_g_0_2': 8.0,
     'ada_b_0_2': 3.962,
     'a_sinks_0_2': 8.0,
     'norm_g_1_2': 8.0,
     'ada_b_1_2': 5.299,
     'b_q_norm_1_2': 8.0,
     'b_kv_norm_1_2': 8.0}
    for name, (base, spread) in spreads.items():
        noise = np.random.default_rng([zlib.crc32(name.encode()), seed]).standard_normal(out[name].shape)
        drawn = base * np.exp(spread * noise) if base else spread * noise
        out[name] = __import__('jax').numpy.asarray(drawn.astype(out[name].dtype))
    for name, factor in factors.items():
        out[name] = (out[name] * factor).astype(out[name].dtype)
    return out
```

```python
import concourse.bass as bass
from concourse import mybir
from contextlib import ExitStack

F32 = mybir.dt.float32
F32R = mybir.dt.float32r
U8 = mybir.dt.uint8
ACT = mybir.ActivationFunctionType
ALU = mybir.AluOpType
AX = mybir.AxisListType

P = 128
D = 1024
KT = D // P
S = 512
NT = S // P
C = 256
HEADS = 8
PAIRS = HEADS // 2
GCH = 8
STRIP = 256
RMS_EPS = 1e-6
LN_EPS = 1e-5
LB_FLOOR = 1e-20
GELU_A = 2.0 * 0.7978845608028654
GELU_B = GELU_A * 0.044715

HEAD_STRIPS = ("q", "v", "ff", "ada", "fb", "i", "ga", "ada")
GATE_STRIPS = ("u|gb", "ada", "u|gb", "ada")
MERGE_STRIPS = ("ma", "pa", "ada", "mb", "pb", "ada")
OUT_STRIPS = ("o", "o")

BUSY = (5, 3)
A_HEADS, A_KV, A_HD, A_GROUP = 16, 4, 64, 4
B_HEADS, B_NOPE, B_ROPE, B_V, B_QR, B_KVR = 16, 64, 32, 64, 256, 128
B_QK = B_NOPE + B_ROPE
ALL = C + S
NC = C // P
BLK = 128
NEG_INF = -1e30
EPS = 1e-6


class Phase:

    def __init__(self, before, iters, strips, counted=True):
        self.iters, self.strips = iters, strips
        self.split = [i for i, s in enumerate(strips) if s != "ada"]
        self.n0 = before.n0 + before.iters * len(before.strips) if before else 0
        self.k0 = before.k0 + before.iters * len(before.split) if before else 0
        self.a0 = before.a0 + before.iters * (len(before.strips) - len(before.split)) if before else 0
        self.per = 2 * len(self.split) if counted else 0
        self.t0 = before.t0 + before.iters * before.per if before else 0
        assert len(strips) % 2 == 0 and len(self.split) % 2 == 0
        self.last = before.strips[-2:] if before else ()

    def n(self, it, s):
        return len(self.strips) * it + (self.n0 + s)

    def k(self, it, s):
        return len(self.split) * it + (self.k0 + sum(i < s for i in self.split))

    def t(self, it, s):
        return self.per * it + (self.t0 + 2 * sum(i < s for i in self.split) * (self.per > 0))

    def w(self, s):
        return sum(i < s for i in self.split) % 2

    def j(self, s):
        return sum(i < s and i not in self.split for i in range(len(self.strips)))

    def a(self, it, s):
        m = len(self.strips) - len(self.split)
        return m * it + (self.a0 + sum(i < s and i not in self.split for i in range(len(self.strips))))


def block_kernel(nc, t):
    ctx = ExitStack()
    with ctx:
        place = {"at": (nc.sbuf_base + 63) // 64 * 64}

        def at(name, shape, dtype, offset):
            return nc.alloc_sbuf_tensor_at(name, shape, dtype, offset=offset)

        def region(nbytes):
            start = place["at"]
            place["at"] += (nbytes + 31) // 32 * 32
            assert place["at"] <= nc.sbuf_usable_end, place["at"] - nc.sbuf_usable_end
            return start

        KB = 1024
        r_raw, r_w = region(16 * KB), region(32 * KB)
        r_h, r_ya, r_yb = region(32 * KB), region(32 * KB), region(32 * KB)
        raw = at("raw", [P, 2, 2048], F32, r_raw)
        w_hi = at("w_hi", [P, 2, 2048], F32R, r_w)
        w_lo = at("w_lo", [P, 2, 2048], F32R, r_w + 16 * KB)
        h_hi = at("h_hi", [P, KT, S], F32R, r_h)
        h_lo = at("h_lo", [P, KT, S], F32R, r_h + 16 * KB)
        ya_hi = at("ya_hi", [P, KT, S], F32R, r_ya)
        ya_lo = at("ya_lo", [P, KT, S], F32R, r_ya + 16 * KB)
        yb_hi = at("yb_hi", [P, KT, S], F32R, r_yb)
        yb_lo = at("yb_lo", [P, KT, S], F32R, r_yb + 16 * KB)
        qf = at("qf", [P, 2, S], F32, r_ya)
        qb = at("qb", [P, 2, S], F32, r_ya + 4 * KB)
        kf = at("kf", [P, 2, S], F32, r_ya + 8 * KB)
        kb = at("kb", [P, 2, S], F32, r_ya + 12 * KB)
        a_diag = at("a_diag", [P, 2, NT, P], F32, r_ya + 16 * KB)
        a_128 = at("a_128", [P, 2, NT, P], F32, r_ya + 20 * KB)
        a_256 = at("a_256", [P, 2, NT, 2 * P], F32, r_ya + 24 * KB)
        q_new = at("q_new", [P, 2, S], F32, r_yb)
        kf_new = at("kf_new", [P, 2, S], F32, r_yb + 4 * KB)
        ln_w_all = at("ln_w_all", [P, D], F32, r_yb + 8 * KB)
        ln_b_all = at("ln_b_all", [P, D], F32, r_yb + 12 * KB)
        kb_new = at("kb_new", [P, 2, S], F32, r_yb + 16 * KB)
        f_f = at("f_f", [P, 2, S], F32, r_yb + 20 * KB)
        f_b = at("f_b", [P, 2, S], F32, r_yb + 24 * KB)
        k_sum = at("k_sum", [P, 2, S], F32, r_yb + 28 * KB)
        tot_a = at("tot_a", [P, 2, S], F32, r_yb + 28 * KB)
        r_vs = region(16 * KB)
        r_y = region(16 * KB)
        r_tmp = region(8 * KB)
        r_s = region(20 * KB)
        r_mv = region(32 * 4)
        vs = at("vs", [P, NT, D], F32, r_vs)
        x_tok = at("x_tok", [P, NT, D], F32, r_vs)
        xT = at("xT", [P, KT, S], F32, r_y)
        y_a = at("y_a", [P, KT, S], F32, r_y)
        tmp = at("tmp", [P, 4, S], F32, r_tmp)
        v_tok = at("v_tok", [P, NT, 2 * P], F32, r_s)
        g_a = at("g_a", [P, 2, S], F32, r_s + 4 * KB)
        tot_b = at("tot_b", [P, 2, C], F32, r_s + 8 * KB)
        u_g = at("u_g", [P, S], F32, r_s + 10 * KB)
        bs_all = at("bs_all", [P, GCH, P], F32, r_s + 12 * KB)
        wsT = at("wsT", [P, GCH, P], F32, r_s + 16 * KB)
        ident = at("ident", [P, P], F32, region(512))
        merged = at("merged", [P, KT, S], F32, r_vs)
        hc_hi = at("hc_hi", [P, KT, C], F32R, r_yb)
        hc_lo = at("hc_lo", [P, KT, C], F32R, r_yb + 8 * KB)
        yc_hi = at("yc_hi", [P, KT, C], F32R, r_yb + 16 * KB)
        yc_lo = at("yc_lo", [P, KT, C], F32R, r_yb + 24 * KB)
        q_all = at("q_all", [P, KT, ALL], F32, r_ya)
        va = at("va", [P, NC + NT, A_KV * A_HD], F32, r_ya + 24 * KB)
        k_all = at("k_all", [P, A_KV, ALL], F32, r_yb + 16 * KB)
        g_lat = at("g_lat", [P, KT, S], F32, r_vs)
        g_ctx = at("g_ctx", [P, KT, C], F32, r_s)
        c_tok = at("c_tok", [P, NC, D], F32, r_vs)
        xcT = at("xcT", [P, KT, C], F32, r_s + 8 * KB)
        cos_a = at("cos_a", [P, S], F32, r_s + 16 * KB)
        sin_a = at("sin_a", [P, S], F32, r_s + 18 * KB)
        mask_a = at("mask_a", [P, C + 3 * BLK], F32, r_s + 16 * KB)
        o_tok = at("o_tok", [P, NC + NT, D], F32, r_h)
        q_st = at("q_st", [P, 2, ALL], F32, r_h + 24 * KB)
        k_st = at("k_st", [P, ALL], F32, r_yb)
        prob_a = at("prob_a", [P, 2, ALL], F32, r_yb + 3 * KB)
        probT_a = at("probT_a", [P, 2, ALL], F32, r_yb + 9 * KB)
        cq_hi = at("cq_hi", [P, 2, S], F32R, r_ya)
        cq_lo = at("cq_lo", [P, 2, S], F32R, r_ya + 4 * KB)
        ckv_hi = at("ckv_hi", [P, ALL], F32R, r_ya + 8 * KB)
        ckv_lo = at("ckv_lo", [P, ALL], F32R, r_ya + 11 * KB)
        cq = at("cq", [P, 2, S], F32, r_ya + 14 * KB)
        ckv = at("ckv", [P, ALL], F32, r_ya + 18 * KB)
        kr = at("kr", [P, ALL], F32, r_ya + 21 * KB)
        cos_b = at("cos_b", [P, S], F32, r_ya + 24 * KB)
        sin_b = at("sin_b", [P, S], F32, r_ya + 26 * KB)
        vb = at("vb", [P, NC + NT, D], F32, r_yb)
        probT_b = at("probT_b", [P, 2, ALL], F32, r_yb + 24 * KB)
        q_b = at("q_b", [P, 2, S], F32, r_h + 16 * KB)
        k_b = at("k_b", [P, 2, ALL], F32, r_h + 20 * KB)
        prob_b = at("prob_b", [P, 2, ALL], F32, r_h + 26 * KB)
        o_b = at("o_b", [P, NT, D], F32, r_h)
        out_tok = at("out_tok", [P, NT, D], F32, r_vs)
        x_again = at("x_again", [P, NT, D], F32, r_s)
        x1T = xT
        ones = at("ones", [P, P], F32, region(512))
        masks = at("masks", [P, 7, P], U8, region(7 * P))
        masks_f = at("masks_f", [P, 7, P], F32, r_ya)
        vec_rows = at("vec_rows", [P, P], F32, r_tmp)
        vec = at("vec", [P, P], F32, region(512))
        ROW, rows = {}, 0
        for name, n in (("norm_w", 8), ("gnorm_w", 1), ("lower_bounds", 16), ("c_2", 8), ("c_ctx_2", 8),
                        ("final_norm_w", 8), ("norm_g_0_2", 8), ("ada_b_0_2", 24), ("norm_g_1_2", 8),
                        ("ada_b_1_2", 24), ("final_g_2", 8), ("b_q_norm_1_2", 2), ("b_kv_norm_1_2", 1)):
            ROW[name] = (rows, n)
            rows += n
        VROWS = rows
        N_CONST = 16 * (2 + len(ROW))

        def cols(name):
            a, n = ROW[name]
            return vec[:, a:a + n]

        lb_raw = at("lb_raw", [P, 2, HEADS], F32, region(64))
        lb_exp = at("lb_exp", [P, 2, HEADS], F32, region(64))
        lb_sum = at("lb_sum", [P, 2, HEADS], F32, region(64))
        lb_soft = at("lb_soft", [P, 2, HEADS], F32, region(64))
        lb = at("lb", [P, 2, HEADS], F32, region(64))
        lb_floor = at("lb_floor", [P, 2, HEADS], F32, region(64))
        lb_rest = at("lb_rest", [P, 2, HEADS], F32, region(64))
        ada = at("ada", [P, 96], F32, region(384))
        c_sig = at("c_sig", [P, 2, KT], F32, region(64))
        c_raw = cols("c_2").tensor[:, ROW["c_2"][0]:ROW["c_2"][0] + 16].rearrange("p (o k) -> p o k", o=2)
        cT = at("cT", [P, KT, 2], F32, region(64))
        v_stat = at("v_stat", [P, NT, 2], F32, r_mv)
        v_rstd = at("v_rstd", [P, NT], F32, r_mv + 32)
        v_bn = at("v_bn", [P, 2, 6], F32, r_mv + 64)
        sink8 = at("sink8", [P, A_HEADS], F32, region(64))
        sink_st = at("sink_st", [P, 2 * A_GROUP], F32, region(32))
        mods = at("mods", [P, 2, KT], F32, region(64))
        a_small = at("a_small", [P, 2, 8], F32, region(64))

        ps = ctx.enter_context(nc.psum_tensor("ps", [P, 8, S], F32))

        def sem(name):
            return ctx.enter_context(nc.semaphore(name))

        s_raw = [sem("s_raw0"), sem("s_raw1")]
        s_hi = sem("s_hi")
        s_lo = sem("s_lo")
        s_proj = sem("s_proj")
        s_ada = sem("s_ada")
        s_adaev = sem("s_adaev")
        s_free = sem("s_free")
        s_sig = sem("s_sig")
        s_pre = sem("s_pre")
        s_const = sem("s_const")
        s_ones = sem("s_ones")
        s_vt = sem("s_vt")
        s_setup = sem("s_setup")
        s_lbx = sem("s_lbx")
        s_x = sem("s_x")
        s_xt = sem("s_xt")
        s_xe = sem("s_xe")
        s_sq = sem("s_sq")
        s_sqm = sem("s_sqm")
        s_ms = sem("s_ms")
        s_rs = sem("s_rs")
        s_h = sem("s_h")
        s_hh = sem("s_hh")
        s_hl = sem("s_hl")
        s_gla = sem("s_gla")
        s_gprep = sem("s_gprep")
        s_gcp_act = sem("s_gcp_act")
        s_gcp_dve = sem("s_gcp_dve")
        s_kcopy = sem("s_kcopy")
        s_ks = sem("s_ks")
        s_osq = sem("s_osq")
        s_gms = sem("s_gms")
        s_grs = sem("s_grs")
        s_y = sem("s_y")
        s_pool = sem("s_pool")
        s_vs = sem("s_vs")
        s_ws = sem("s_ws")
        s_wst = sem("s_wst")
        s_ln = sem("s_ln")
        s_lnp = sem("s_lnp")
        s_mix = sem("s_mix")
        s_yb = sem("s_yb")
        s_ybh = sem("s_ybh")
        s_ybl = sem("s_ybl")
        s_yah = sem("s_yah")
        s_yal = sem("s_yal")
        s_mh = sem("s_mh")
        s_ml = sem("s_ml")
        s_x2 = sem("s_x2")
        s_sigg = sem("s_sigg")
        s_preg = sem("s_preg")
        s_sigm = sem("s_sigm")
        s_m = sem("s_m")
        s_o = sem("s_o")
        s_in2 = sem("s_in2")
        s_taba = sem("s_taba")
        s_mska = sem("s_mska")
        s_tabb = sem("s_tabb")
        s_ct = sem("s_ct")
        s_ctx = sem("s_ctx")
        s_nsq = sem("s_nsq")
        s_nmm = sem("s_nmm")
        s_nms = sem("s_nms")
        s_nrs = sem("s_nrs")
        s_nh = sem("s_nh")
        s_nhh = sem("s_nhh")
        s_nhl = sem("s_nhl")
        s_nx = sem("s_nx")
        s_sig2 = sem("s_sig2")
        s_kk = sem("s_kk")
        s_kd = sem("s_kd")
        s_stage = sem("s_stage")
        s_sc = sem("s_sc")
        s_neg = sem("s_neg")
        s_exp = sem("s_exp")
        s_tr = sem("s_tr")
        s_cpa = sem("s_cpa")
        s_cpd = sem("s_cpd")
        s_pv = sem("s_pv")
        s_oo = sem("s_oo")
        s_ot = sem("s_ot")
        s_og = sem("s_og")
        s_vb = sem("s_vb")
        s_vp = sem("s_vp")
        s_own = sem("s_own")
        s_up = sem("s_up")
        s_upe = sem("s_upe")
        s_ft = sem("s_ft")
        s_fe = sem("s_fe")
        s_dve = sem("s_dve")
        s_out = sem("s_out")
        block = ctx.enter_context(nc.Block())

        w_in = t["w_in"][0, :, :].rearrange("(k p) n -> p k n", p=P)
        IN = {n: i * D for i, n in enumerate(
            ("q", "ff", "fb", "i", "ga", "u", "v", "gb", "ma", "mb"))}
        ada0 = t["ada_w_0_2"].rearrange("(k p) n -> p k n", p=P)
        ada1 = t["ada_w_1_2"].rearrange("(k p) n -> p k n", p=P)
        wpa = t["w_proj_a"][0, :, :].rearrange("(k p) n -> p k n", p=P)
        wpb = t["w_proj_b"][0, :, :].rearrange("(k p) n -> p k n", p=P)
        w_out = t["w_out"][0, :, :].rearrange("(k p) n -> p k n", p=P)
        heads = Phase(None, PAIRS, HEAD_STRIPS)
        gates = Phase(heads, GCH // 2, GATE_STRIPS)
        merge = Phase(gates, KT // 2, MERGE_STRIPS)
        outs = Phase(merge, KT // 4, OUT_STRIPS)
        a_q = Phase(outs, 2, ("q", "q"))
        a_kv = Phase(a_q, 1, ("k", "v"))
        a_g = Phase(a_kv, 2, ("g", "g"))
        a_out = Phase(a_g, 2, ("o", "o"))
        b_in = Phase(a_out, 1, ("cq", "kv"))
        b_g = Phase(b_in, 2, ("g", "g"))
        b_v = Phase(b_g, 1, ("v", "v"), counted=False)
        b_up = Phase(b_v, B_HEADS // 4, ("up", "up"), counted=False)
        b_out = Phase(b_up, 2, ("o", "o"))


        A_UNITS = A_GROUP * (NC + NT)
        B_UNITS = NT

        def a_unit(i):
            if i < NC:
                return [(0, C)], [(0, C)]
            lo, hi = max(i - 1, NC), min(i + 2, NC + NT)
            keys = [(0, C), (lo * P, hi * P)]
            m0 = C if i > NC else C + BLK
            return keys, [(0, C), (m0, m0 + (hi - lo) * P)]

        A_TILES = [(i, h) for i in range(NC + NT) for h in range(A_GROUP)]

        def a_step(g, x):
            gx, y = (g, x) if x >= 0 else (g - 1, x + A_UNITS)
            return A_UNITS * g + x, gx, y, A_TILES[y][0], A_TILES[y][1]

        def blocks_of(keys):
            return [b for a, z in keys for b in range(a // P, z // P)]

        def in_banks(n):
            return {2: 1, 4: 3, 5: 4, 6: 4}[n]

        def score_parts(keys):
            parts, col = [], 0
            for a, z in keys:
                while a < z:
                    n = min(z - a, S - col % S)
                    parts.append((col, a, n))
                    a, col = a + n, col + n
            return parts

        def k_of(a, slot, n=STRIP):
            return a[:, slot, 0:KT * n].rearrange("p (k n) -> p k n", k=KT)

        @block.sync
        def _(sp):
            sp.dma_start(x_tok[:, :, :], t["x"][0, :, :].rearrange("(n p) d -> p n d", p=P)).then_inc(s_x, 16)
            sp.dma_start(ident[:, :], t["ident"]).then_inc(s_const, 16)
            sp.dma_start(masks_f[:, :, :], t["masks"].rearrange("l p s -> p l s")).then_inc(s_const, 16)
            for name, (a, n) in ROW.items():
                flat = t[name]
                while len(flat.shape) > 1:
                    flat = flat.rearrange("a b c -> (a b c)" if len(flat.shape) == 3 else "a b -> (a b)")
                sp.dma_start(vec_rows[a:a + n, :], flat.rearrange("(k p) -> k p", p=P)).then_inc(s_const, 16)

            def load(ph, it, s, src):
                n = ph.n(it, s)
                if s >= 2 or ph.last or not (isinstance(it, int) and it == 0):
                    kinds = (tuple(ph.strips[s - 2:s]) if s >= 2 else
                             tuple(ph.strips[-2:] if not (isinstance(it, int) and it == 0) else ph.last)[s:] + tuple(ph.strips[:s]))
                    splits = sum(k != "ada" for k in kinds)
                    if kinds[0] == "ada":
                        sp.wait_ge(s_ada, ph.a(it, s) - (2 - splits) + 1)
                    else:
                        sp.wait_ge(s_lo, ph.k(it, s) - splits + 1)
                for dst, part in src:
                    sp.dma_start(dst, part).then_inc(s_raw[s % 2], 16 * (2 // len(src)))

            def heads_it(it):
                for s, kind in enumerate(HEAD_STRIPS):
                    c = heads.a(it, s) * STRIP if kind == "ada" else it * STRIP + IN[kind]
                    if not isinstance(it, int):
                        c = sp.snap(c)
                    src = (ada0 if kind == "ada" else w_in)[:, :, bass.ds(c, STRIP)]
                    load(heads, it, s, [(k_of(raw, s % 2), src)])

            sp.dma_start(wsT[:, :, :], t["w_s"][0, :, :, :].rearrange("g t s -> t g s")).then_inc(s_ws, 16)
            heads_it(0)
            sp.dma_start(ln_w_all[:, :], t["ln_w"].partition_broadcast(P)).then_inc(s_lnp, 16)
            sp.dma_start(ln_b_all[:, :], t["ln_b"].partition_broadcast(P)).then_inc(s_lnp, 16)
            sp.dma_start(bs_all[:, :, :].rearrange("p g t -> p (g t)"), t["b_s"].rearrange("o g t -> o (g t)").partition_broadcast(P)).then_inc(s_lnp, 16)
            with sp.Fori(1, PAIRS) as it:
                heads_it(it)

            def ada_cols(ph, it, s):
                n = ph.a(it, s)
                return (ada0 if n < 12 else ada1)[:, :, n % 12 * STRIP:(n % 12 + 1) * STRIP]

            for it in range(gates.iters):
                for s, kind in enumerate(GATE_STRIPS):
                    if kind == "ada":
                        load(gates, it, s, [(k_of(raw, s % 2), ada_cols(gates, it, s))])
                    else:
                        g = 2 * it + s // 2
                        load(gates, it, s, [(k_of(raw, s % 2)[:, :, h * P:(h + 1) * P],
                                             w_in[:, :, IN[n] + g * P:IN[n] + (g + 1) * P]) for h, n in enumerate(("u", "gb"))])

            def merge_it(it):
                c, ca = it * STRIP, 2 * it * STRIP
                for s, kind in enumerate(MERGE_STRIPS):
                    if kind == "ada":
                        src = ada1[:, :, bass.ds(ca + (4 + merge.j(s)) * STRIP, STRIP)]
                    elif kind in ("ma", "mb"):
                        src = w_in[:, :, bass.ds(c + IN[kind], STRIP)]
                    else:
                        src = (wpa if kind == "pa" else wpb)[:, :, bass.ds(c, STRIP)]
                    load(merge, it, s, [(k_of(raw, s % 2), src)])
            merge_it(0)
            sp.wait_ge(s_yb, GCH)
            sp.wait_ge(s_mix, GCH)
            sp.dma_start(x_again[:, :, :], t["x"][0, :, :].rearrange("(n p) d -> p n d", p=P)).then_inc(s_x2, 16)
            for it in range(1, merge.iters):
                merge_it(it)
            for it in range(outs.iters):
                for s in range(2):
                    load(outs, it, s, [(k_of(raw, s % 2), w_out[:, :, (2 * it + s) * STRIP:(2 * it + s + 1) * STRIP])])

            sp.wait_ge(s_mh, KT)
            sp.wait_ge(s_ml, KT)
            sp.dma_start(c_tok[:, :, :], t["ctx_2"][0, :, :].rearrange("(n p) d -> p n d", p=P)).then_inc(s_in2, 16)
            sp.wait_ge(s_xt, 2 * KT)
            sp.dma_start(cos_a[:, :], t["cos_a"]).then_inc(s_taba, 16)
            sp.dma_start(sin_a[:, :], t["sin_a"]).then_inc(s_taba, 16)
            sp.dma_start(sink8[:, :], t["a_sinks_0_2"].partition_broadcast(P)).then_inc(s_taba, 16)

            def cols_of(w, c, n=STRIP):
                return w.rearrange("(k p) n -> p k n", p=P)[:, :, c:c + n]

            def plain(ph, w, c0):
                for it in range(ph.iters):
                    for s in range(2):
                        load(ph, it, s, [(k_of(raw, s % 2), cols_of(w, c0 + (2 * it + s) * STRIP))])

            plain(a_q, t["a_w_in_0_2"], 0)
            plain(a_kv, t["a_w_in_0_2"], A_HEADS * A_HD)
            plain(a_g, t["a_w_in_0_2"], A_HEADS * A_HD + 2 * A_KV * A_HD)
            sp.wait_ge(s_free, a_g.t0)
            sp.dma_start(mask_a[:, :], t["mask_a"]).then_inc(s_mska, 16)
            plain(a_out, t["a_w_o_0_2"], 0)
            load(b_in, 0, 0, [(k_of(raw, 0), cols_of(t["b_w_in_1_2"], 0))])
            load(b_in, 0, 1, [(k_of(raw, 1, B_KVR + B_ROPE), cols_of(t["b_w_in_1_2"], B_QR, B_KVR + B_ROPE))])
            plain(b_g, t["b_w_in_1_2"], B_QR + B_KVR + B_ROPE)
            sp.wait_ge(s_free, b_in.t0)
            sp.dma_start(cos_b[0:B_QK, :], t["cos_b"]).then_inc(s_tabb, 16)
            sp.dma_start(sin_b[0:B_QK, :], t["sin_b"]).then_inc(s_tabb, 16)
            for s in range(2):
                load(b_v, 0, s, [(raw[:, s, 0:D], t["b_w_ukv_1_2"][:, s * D:(s + 1) * D])])
            uq = t["b_w_uq_1_2"].rearrange("(k p) n -> p k n", p=P)
            for it in range(b_up.iters):
                for s in range(2):
                    h0 = 2 * (2 * it + s)
                    load(b_up, it, s, [(raw[:, s, 0:4 * B_QK].rearrange("p (k n) -> p k n", k=2), uq[:, :, h0 * B_QK:(h0 + 2) * B_QK]),
                                       (raw[:, s, 4 * B_QK:4 * B_QK + 2 * P], t["b_w_ukv_1_2"][:, h0 * P:(h0 + 2) * P])])
            plain(b_out, t["b_w_o_1_2"], 0)
            for n in range(NT):
                sp.wait_ge(s_fe, 2 * n + 2)
                sp.dma_start(t["out"][0, n * P:(n + 1) * P, :], out_tok[:, n, :]).then_inc(s_out, 16)
            sp.wait_ge(s_out, 16 * NT)

        @block.scalar
        def _(act):
            def hi(ph, it, s, used=None):
                act.wait_ge(s_raw[s % 2], 16 * ph.n(it, s) + 32 - 16 * (s % 2))
                done = ph.t(it, s) - 2
                if used:
                    act.wait_ge(*used)
                elif not (isinstance(done, int) and done <= 0):
                    act.wait_ge(s_proj, done)
                nc.scalar.activation(w_hi[:, ph.w(s), :], raw[:, s % 2, :], ACT.Copy).then_inc(s_hi, 1)

            act.wait_ge(s_lbx, 1)
            nc.scalar.activation(lb_exp[:, :, :], lb_raw[:, :, :], ACT.Exp).then_inc(s_lbx, 1)
            for k in range(KT):
                act.wait_ge(s_xt, k + 1)
                nc.scalar.activation(xT[:, k, :], ps[:, k % 2, :], ACT.Copy).then_inc(s_xe, 1)
                act.wait_ge(s_xe, k + 1)
                if k >= 2:
                    act.wait_ge(s_sqm, k - 1)
                nc.scalar.activation(tmp[:, k % 2, :], xT[:, k, :], ACT.Square).then_inc(s_sq, 1)
            hi(heads, 0, 0)
            act.wait_ge(s_ms, 1)
            nc.scalar.activation(tmp[:, 3, :], tmp[:, 2, :], ACT.Sqrt).then_inc(s_rs, 1)
            for k in range(KT):
                act.wait_ge(s_h, k + 1)
                nc.scalar.activation(h_hi[:, k, :], tmp[:, k % 2, :], ACT.Copy).then_inc(s_hh, 1)
            act.wait_ge(s_wst, 1)
            nc.scalar.activation(wsT[:, :, :].rearrange("p g s -> p (g s)"), ps[:, 4:6, :].rearrange("p a s -> p (a s)"), ACT.Copy).then_inc(s_wst, 1)
            nc.scalar.activation(c_sig[:, :, :], c_raw, ACT.Sigmoid).then_inc(s_setup, 1)

            def head_tiles(it, first):
                sig = 13 * it
                for s, kind in enumerate(HEAD_STRIPS):
                    if kind == "ada":
                        act.wait_ge(s_ada, heads.a(it, s) + 1)
                        nc.scalar.activation(ada[:, bass.ds(4 * heads.a(it, s), 4)],
                                             ps[:, 6 + heads.j(s), 0:4], ACT.Copy).then_inc(s_adaev, 1)
                        continue
                    x = heads.split.index(s)
                    if x + 1 < NSPLIT_H:
                        hi(heads, it, heads.split[x + 1])
                    else:
                        hi(heads, it + 1, 0)
                    for j in range(2):
                        tt = 2 * x + j
                        if not first:
                            gla_act(it - 1, tt)
                        act.wait_ge(s_proj, heads.t(it, s) + j + 1)
                        bank, a, b = ps[:, j, :], tmp[:, 2 * j, :], tmp[:, 2 * j + 1, :]
                        if kind != "i" and not (first and s == 0):
                            act.wait_ge(s_free, heads.t(it, s) + j - 1)
                        if kind == "v":
                            nc.scalar.activation(a, bank, ACT.Square).then_inc(s_sig, 1)
                            act.wait_ge(s_pre, 2 * it + j + 1)
                            nc.scalar.activation(a, b, ACT.Sigmoid).then_inc(s_sig, 1)
                        elif kind in ("ff", "fb"):
                            nc.scalar.activation(a, bank, ACT.Sigmoid)
                            nc.scalar.activation(b, bank, ACT.Sigmoid, scale=-1.0).then_inc(s_sig, 1)
                        elif kind in ("q", "ga"):
                            nc.scalar.activation(a, bank, ACT.Sigmoid).then_inc(s_sig, 1)

            def gla_act(g, tt):
                if tt == 0:
                    act.wait_ge(s_ks, g + 1)
                    act.wait_ge(s_y, g + 1)
                    nc.scalar.activation(kf[:, :, :], kf_new[:, :, :], ACT.Copy)
                    nc.scalar.activation(kb[:, :, :], kb_new[:, :, :], ACT.Copy).then_inc(s_kcopy, 1)
                    act.wait_ge(s_gla, 12 * g + 1)
                    nc.scalar.activation(a_diag[:, :, :, :].rearrange("p h n s -> p (h n s)"),
                                         ps[:, 2:4, :].rearrange("p a s -> p (a s)"), ACT.Copy).then_inc(s_gcp_act, 1)
                if tt == 7:
                    act.wait_ge(s_gla, 12 * g + 9)
                    nc.scalar.activation(a_128[:, :, :, :].rearrange("p h n s -> p (h n s)"),
                                         ps[:, 2:4, :].rearrange("p a s -> p (a s)"), ACT.Copy).then_inc(s_gcp_act, 1)
                if tt == 8:
                    act.wait_ge(s_gla, 12 * g + 10)
                    nc.scalar.activation(a_256[:, :, :, :].rearrange("p h n s -> p (h n s)"),
                                         ps[:, 2:6, :].rearrange("p a s -> p (a s)"), ACT.Copy).then_inc(s_gcp_act, 1)
                if tt == 9:
                    act.wait_ge(s_gla, 12 * g + 11)
                    nc.scalar.activation(qf[:, :, :], ps[:, 2:4, :], ACT.Square).then_inc(s_osq, 1)
                if tt == 10:
                    act.wait_ge(s_gms, g + 1)
                    nc.scalar.activation(qb[:, :, :], kf[:, :, :], ACT.Sqrt).then_inc(s_grs, 1)

            head_tiles(0, True)
            with act.Fori(1, PAIRS) as it:
                head_tiles(it, False)

            def ada_out(ph, it, s, bank):
                act.wait_ge(s_ada, ph.a(it, s) + 1)
                nc.scalar.activation(ada[:, bass.ds(4 * ph.a(it, s), 4)], ps[:, bank, 0:4], ACT.Copy).then_inc(s_adaev, 1)

            def split_y(g):
                act.wait_ge(s_yb, g + 1)
                nc.scalar.activation(yb_hi[:, g, :], tmp[:, 3, :], ACT.Copy).then_inc(s_ybh, 1)

            g_last = PAIRS - 1
            for g in range(GCH):
                it, s = g // 2, 2 * (g % 2)
                for j in range(2):
                    tt = 2 * g + j
                    if tt <= 10:
                        gla_act(g_last, tt)
                    if tt == 0:
                        act.wait_ge(s_ln, 1)
                        nc.scalar.activation(v_rstd[:, :], v_stat[:, :, 1], ACT.Sqrt).then_inc(s_ln, 1)
                    if j == 0:
                        nxt = (gates, it, 2) if s == 0 else (gates, it + 1, 0) if it + 1 < gates.iters else (merge, 0, 0)
                        hi(*nxt)
                        if g:
                            split_y(g - 1)
                    if tt >= 12:
                        act.wait_ge(s_y, PAIRS + 1)
                        for k in (2 * (tt - 12), 2 * (tt - 12) + 1):
                            nc.scalar.activation(ya_hi[:, k, :], y_a[:, k, :], ACT.Copy).then_inc(s_yah, 1)
                    act.wait_ge(s_proj, gates.t(it, s) + j + 1)
                    if j == 0:
                        act.wait_ge(s_free, gates.t(it, s) - 1)
                        nc.scalar.activation(tmp[:, 0, :], ps[:, 0, :], ACT.Square).then_inc(s_sigg, 1)
                        act.wait_ge(s_preg, g + 1)
                        nc.scalar.activation(tmp[:, 0, :], tmp[:, 1, :], ACT.Sigmoid).then_inc(s_sigg, 1)
                    else:
                        act.wait_ge(s_free, gates.t(it, s))
                        nc.scalar.activation(tmp[:, 2, :], ps[:, 1, :], ACT.Sigmoid).then_inc(s_sigg, 1)
                ada_out(gates, it, s + 1, 6)
            split_y(GCH - 1)

            def merge_act(it):
                for s, kind in enumerate(MERGE_STRIPS):
                    if kind == "ada":
                        ada_out(merge, it, s, 7 - merge.j(s))
                        continue
                    x = merge.split.index(s)
                    if x < 3:
                        hi(merge, it, merge.split[x + 1])
                    else:
                        hi(merge, it + 1, 0)
                    if kind in ("ma", "mb"):
                        for j in range(2):
                            act.wait_ge(s_proj, merge.t(it, s) + j + 1)
                            act.wait_ge(s_free, merge.t(it, s) + j - 1)
                            nc.scalar.activation(tmp[:, x + j, :], ps[:, j, :], ACT.Sigmoid).then_inc(s_sigm, 1)
            act.wait_ge(s_ybl, GCH)
            with act.Fori(0, merge.iters) as it:
                merge_act(it)

            act.wait_ge(s_proj, outs.t0)
            for k in range(KT):
                act.wait_ge(s_m, k // 2 + 1)
                nc.scalar.activation(h_hi[:, k, :], merged[:, k, :], ACT.Copy).then_inc(s_mh, 1)
            act.wait_ge(s_yal, KT)
            for k in range(KT):
                act.wait_ge(s_xt, KT + k + 1)
                nc.scalar.activation(xT[:, k, :], ps[:, 2 + k % 4, :], ACT.Copy).then_inc(s_xe, 1)
                if k == 1:
                    hi(outs, 0, 1)
            hi(outs, 1, 0)

            for k in range(KT):
                act.wait_ge(s_ct, k + 1)
                nc.scalar.activation(xcT[:, k, :], ps[:, 6 + k % 2, 0:C], ACT.Copy).then_inc(s_ctx, 1)
            cnt = {"sq": 0, "n": 0, "h": 0}

            def pair(k):
                return tmp[:, 2 * (k % 2):2 * (k % 2) + 2, :].rearrange("p a s -> p (a s)")

            def norm(srcs, ready, n):
                for k, parts in enumerate(srcs):
                    if ready[k]:
                        act.wait_ge(*ready[k])
                    if k >= 2:
                        act.wait_ge(s_nmm, cnt["sq"] - 1)
                    o = 0
                    for src in parts:
                        w = src.shape[-1]
                        sq = tmp[:, k % 2, :] if n <= S else pair(k)
                        last = nc.scalar.activation(sq[:, o:o + w], src, ACT.Square)
                        o += w
                    cnt["sq"] += 1
                    last.then_inc(s_nsq, 1)
                cnt["n"] += 1
                act.wait_ge(s_nms, cnt["n"])
                nc.scalar.activation(pair(1)[:, 0:n], pair(0)[:, 0:n], ACT.Sqrt).then_inc(s_nrs, 1)

            def parts(hi_of):
                for k, (dst, src) in enumerate(hi_of):
                    cnt["h"] += 1
                    act.wait_ge(s_nh, cnt["h"])
                    nc.scalar.activation(dst, src, ACT.Copy).then_inc(s_nhh, 1)

            hi(outs, 1, 1)
            act.wait_ge(s_ctx, KT)
            norm([[xcT[:, k, :]] for k in range(KT)], [None] * KT, C)
            parts([(hc_hi[:, k, :], tmp[:, k % 2, 0:C]) for k in range(KT)])
            hi(a_q, 0, 0)
            act.wait_ge(s_nhl, KT)
            norm([[x1T[:, k, :]] for k in range(KT)], [(s_free, outs.t0 + k + 1) for k in range(KT)], S)
            norm([[x1T[:, k, :]] for k in range(KT)], [(s_nx, k + 1) for k in range(KT)], S)
            parts([(h_hi[:, k, :], tmp[:, k % 2, :]) for k in range(KT)])
            act.wait_ge(s_nhl, 2 * KT)

            def order(phases):
                return [(ph, it, s) for ph in phases for it in range(ph.iters) for s in range(len(ph.split))]

            def gate_sig(ph, it, s, j, ctx_):
                act.wait_ge(s_proj, ph.t(it, s) + j + 1)
                act.wait_ge(s_free, ph.t(it, s) + j - 1)
                a = 2 * j if ctx_ else j
                last = nc.scalar.activation(pair(j)[:, 0:S], ps[:, a, :], ACT.Sigmoid)
                if ctx_:
                    last = nc.scalar.activation(pair(j)[:, S:ALL], ps[:, a + 1, 0:C], ACT.Sigmoid)
                last.then_inc(s_sig2, 1)

            seq = order([a_q, a_kv, a_g, a_out])
            for n, (ph, it, s) in enumerate(seq):
                if ph is a_out:
                    break
                if n + 1 < len(seq):
                    hi(*seq[n + 1])
                if ph is a_kv and s == 0:
                    for j in range(2):
                        act.wait_ge(s_kk, j + 1)
                        for hh in range(2):
                            for d in range(2):
                                last = nc.scalar.activation(k_all[d * A_HD:(d + 1) * A_HD, 2 * j + hh, :],
                                                            pair(j)[hh * A_HD:(hh + 1) * A_HD, 0:ALL], ACT.Copy)
                        last.then_inc(s_kd, 1)
                if ph is a_g:
                    for j in range(2):
                        gate_sig(ph, it, s, j, True)

            def exps(u, x, prob, src, scale, small, sink=None):
                act.wait_ge(s_neg, u + 1)
                if sink is not None:
                    nc.scalar.activation(small[:, x % 2, 3:4], sink, ACT.Exp, bias=small[:, x % 2, 1:2])
                n = src.shape[-1]
                nc.scalar.activation(prob[:, x % 2, 0:n], src, ACT.Exp, bias=small[:, x % 2, 1:2], scale=scale,
                                     accum_out=small[:, x % 2, 2:3]).then_inc(s_exp, 1)

            def turned(u, x, n, pT):
                act.wait_ge(s_tr, u + 1)
                if not (isinstance(u, int) and u < 2):
                    act.wait_ge(s_pv, u - 1)
                w = in_banks(n) * P
                nc.scalar.activation(pT[:, x % 2, 0:w], ps[:, 4, 0:w], ACT.Copy).then_inc(s_cpa, 1)

            def a_group(g, xs, first=False):
                for x in xs:
                    if not (first and x < 1):
                        u, _, y, i, _ = a_step(g, x - 1)
                        turned(u, y, len(blocks_of(a_unit(i)[0])), probT_a)
                    if x < A_UNITS:
                        u, _, y, i, h = a_step(g, x)
                        n = sum(z - a for a, z in a_unit(i)[0])
                        exps(u, y, prob_a, prob_a[:, y % 2, 0:n], float(A_HD) ** -0.5, a_small, sink_st[:, h:h + 1])
            act.wait_ge(s_free, a_out.t0)
            a_group(0, range(A_UNITS), True)
            with act.Fori(1, A_KV) as g:
                a_group(g, range(A_UNITS))
            a_group(A_KV - 1, (A_UNITS,))
            gated = [(ya_hi[:, k, :], pair(k)[:, 0:S], yc_hi[:, k, :], pair(k)[:, S:ALL]) for k in range(KT)]
            for a, b, c, d in gated:
                cnt["h"] += 1
                act.wait_ge(s_nh, cnt["h"])
                nc.scalar.activation(a, b, ACT.Copy)
                nc.scalar.activation(c, d, ACT.Copy).then_inc(s_nhh, 1)
            for n in range(1, 4):
                hi(a_out, n // 2, n % 2)
            hi(b_in, 0, 0)
            hi(b_in, 0, 1)
            act.wait_ge(s_free, b_in.t0)
            act.wait_ge(s_nhl, 3 * KT)
            norm([[x1T[:, k, :]] for k in range(KT)], [None] * KT, S)
            parts([(h_hi[:, k, :], tmp[:, k % 2, :]) for k in range(KT)])
            act.wait_ge(s_nhl, 4 * KT)
            norm([[xcT[:, k, :]] for k in range(KT)], [None] * KT, C)
            parts([(hc_hi[:, k, :], tmp[:, k % 2, 0:C]) for k in range(KT)])
            hi(b_g, 0, 0)
            act.wait_ge(s_nhl, 5 * KT)
            norm([[cq[:, k, :]] for k in range(2)], [(s_free, b_in.t0 + k + 1) for k in range(2)], S)
            parts([(cq_hi[:, k, :], tmp[:, k, :]) for k in range(2)])
            act.wait_ge(s_nhl, 5 * KT + 2)
            hi(b_g, 0, 1)
            norm([[ckv[:, :]]], [(s_free, b_in.t0 + 3)], ALL)
            parts([(ckv_hi[:, :], pair(0)[:, 0:ALL])])
            act.wait_ge(s_nhl, 5 * KT + 3)
            seq = order([b_g])
            for n, (ph, it, s) in enumerate(seq):
                if n + 1 == len(seq):
                    hi(b_v, 0, 0)
                elif n:
                    hi(*seq[n + 1])
                for j in range(2):
                    gate_sig(ph, it, s, j, False)
            hi(b_v, 0, 1, (s_proj, b_v.t0))
            for m in range(2):
                hi(b_up, 0, m, (s_vb, (NC + NT) * (m + 1)))
            units = [(h, i) for h in range(B_HEADS) for i in range(NT)]
            A_ALL = A_KV * A_UNITS
            for x in range(len(units) + 1):
                u = A_ALL + x
                if x >= 1:
                    turned(u - 1, x - 1, NC + NT, probT_b)
                if x < len(units):
                    h, i = units[x]
                    exps(u, x, prob_b, ps[:, 2 * (x % 2):2 * (x % 2) + 2, :].rearrange("p a s -> p (a s)")[:, 0:ALL],
                         B_QK ** -0.5, a_small)
                    if h % 2 == 0 and i == 0 and 2 <= h // 2 + 1 < B_HEADS // 2:
                        m = h // 2 + 1
                        hi(b_up, m // 2, m % 2, (s_upe, 6 * (m - 1)))
            hi(b_out, 0, 0, (s_upe, 6 * 7))
            hi(b_out, 0, 1, (s_upe, 6 * 8))
            for k in range(KT):
                cnt["h"] += 1
                act.wait_ge(s_nh, cnt["h"])
                nc.scalar.activation(ya_hi[:, k, :], pair(k)[:, 0:S], ACT.Copy).then_inc(s_nhh, 1)
            for n in range(2, 4):
                hi(b_out, n // 2, n % 2)
            act.wait_ge(s_nhl, 6 * KT + 3)
            norm([[x1T[:, k, :]] for k in range(KT)], [(s_free, b_out.t0 + k + 1) for k in range(KT)], S)
            for n in range(NT):
                for h in range(2):
                    x = 2 * n + h
                    act.wait_ge(s_ft, x + 1)
                    nc.scalar.activation(out_tok[:, n, h * S:(h + 1) * S], ps[:, 4 + x % 2, :], ACT.Copy).then_inc(s_fe, 1)

        @block.gpsimd
        def _(pool):
            def lo(ph, it, s):
                pool.wait_ge(s_hi, ph.k(it, s) + 1)
                nc.gpsimd.tensor_tensor(w_lo[:, ph.w(s), :], raw[:, s % 2, :], w_hi[:, ph.w(s), :].bitcast(F32),
                                        ALU.subtract).then_inc(s_lo, 1)

            nc.gpsimd.memset(ones[:, :], 1.0).then_inc(s_ones, 1)
            lo(heads, 0, 0)
            for k in range(KT):
                pool.wait_ge(s_hh, k + 1)
                nc.gpsimd.tensor_tensor(h_lo[:, k, :], tmp[:, k % 2, :], h_hi[:, k, :].bitcast(F32),
                                        ALU.subtract).then_inc(s_hl, 1)
            for s in heads.split[1:]:
                lo(heads, 0, s)
            with pool.Fori(1, PAIRS) as it:
                for s in heads.split:
                    lo(heads, it, s)

            lo(gates, 0, 0)
            pool.wait_ge(s_lnp, 48)
            for n in range(NT):
                pool.wait_ge(s_ln, 3 + n)
                nc.gpsimd.tensor_tensor(vs[:, n, :], vs[:, n, :], ln_w_all[:, :], ALU.mult).then_inc(s_pool, 1)
                pool.wait_ge(s_pool, n + 1)
                nc.gpsimd.tensor_tensor(vs[:, n, :], vs[:, n, :], ln_b_all[:, :], ALU.add).then_inc(s_vs, 1)
                if n == 1:
                    lo(gates, 0, 2)

            def split_y(g):
                pool.wait_ge(s_ybh, g + 1)
                nc.gpsimd.tensor_tensor(yb_lo[:, g, :], tmp[:, 3, :], yb_hi[:, g, :].bitcast(F32), ALU.subtract).then_inc(s_ybl, 1)

            for g in range(GCH):
                if g:
                    split_y(g - 1)
                if 1 <= g < GCH - 1:
                    lo(gates, (g + 1) // 2, 2 * ((g + 1) % 2))
                elif g:
                    lo(merge, 0, 0)
                if g >= 6:
                    for k in range(4 * (g - 6), 4 * (g - 6) + 4):
                        pool.wait_ge(s_yah, k + 1)
                        nc.gpsimd.tensor_tensor(ya_lo[:, k, :], y_a[:, k, :], ya_hi[:, k, :].bitcast(F32), ALU.subtract).then_inc(s_yal, 1)
            split_y(GCH - 1)
            with pool.Fori(0, merge.iters) as it:
                for s in merge.split[1:]:
                    lo(merge, it, s)
                lo(merge, it + 1, 0)
            for k in range(KT):
                pool.wait_ge(s_mh, k + 1)
                nc.gpsimd.tensor_tensor(h_lo[:, k, :], merged[:, k, :], h_hi[:, k, :].bitcast(F32), ALU.subtract).then_inc(s_ml, 1)
            for n in range(1, 4):
                lo(outs, n // 2, n % 2)

            cnt = {"h": 0}

            def low(parts):
                cnt["h"] += 1
                pool.wait_ge(s_nhh, cnt["h"])
                for dst, src, high in parts:
                    last = nc.gpsimd.tensor_tensor(dst, src, high.bitcast(F32), ALU.subtract)
                last.then_inc(s_nhl, 1)

            def pair(k):
                return tmp[:, 2 * (k % 2):2 * (k % 2) + 2, :].rearrange("p a s -> p (a s)")

            def strips(*phases):
                for ph in phases:
                    for it in range(ph.iters):
                        for s in range(2):
                            lo(ph, it, s)

            for k in range(KT):
                low([(hc_lo[:, k, :], tmp[:, k % 2, 0:C], hc_hi[:, k, :])])
            lo(a_q, 0, 0)
            for k in range(KT):
                low([(h_lo[:, k, :], tmp[:, k % 2, :], h_hi[:, k, :])])
            lo(a_q, 0, 1)
            lo(a_q, 1, 0)
            lo(a_q, 1, 1)
            strips(a_kv, a_g)
            lo(a_out, 0, 0)
            for k in range(KT):
                low([(ya_lo[:, k, :], pair(k)[:, 0:S], ya_hi[:, k, :]), (yc_lo[:, k, :], pair(k)[:, S:ALL], yc_hi[:, k, :])])
            for n in range(1, 4):
                lo(a_out, n // 2, n % 2)
            lo(b_in, 0, 0)
            lo(b_in, 0, 1)
            for k in range(KT):
                low([(h_lo[:, k, :], tmp[:, k % 2, :], h_hi[:, k, :])])
            for k in range(KT):
                low([(hc_lo[:, k, :], tmp[:, k % 2, 0:C], hc_hi[:, k, :])])
            lo(b_g, 0, 0)
            for k in range(2):
                low([(cq_lo[:, k, :], tmp[:, k, :], cq_hi[:, k, :])])
            lo(b_g, 0, 1)
            low([(ckv_lo[:, :], pair(0)[:, 0:ALL], ckv_hi[:, :])])
            for n in range(2, 4):
                lo(b_g, n // 2, n % 2)
            strips(b_v, b_up)
            lo(b_out, 0, 0)
            lo(b_out, 0, 1)
            for k in range(KT):
                low([(ya_lo[:, k, :], pair(k)[:, 0:S], ya_hi[:, k, :])])
            for n in range(2, 4):
                lo(b_out, n // 2, n % 2)

        @block.vector
        def _(dve):
            v = nc.vector
            chain = {"n": 0}

            def link(ins):
                chain["n"] = chain["n"] + 1
                ins.then_inc(s_dve, 1)
                dve.wait_ge(s_dve, chain["n"])

            dve.sem_inc(s_y, 1)
            dve.wait_ge(s_vt, 1)
            link(v.tensor_copy(vec[:, 0:VROWS], ps[:, 3, 0:VROWS]))
            link(v.tensor_copy(masks[:, :, :], masks_f[:, :, :]))
            lbs = cols("lower_bounds").rearrange("p (a k) -> p a k", a=2)
            v.tensor_tensor(lb_raw[:, :, :], lbs, lbs, ALU.subtract).then_inc(s_lbx, 1)
            dve.wait_ge(s_lbx, 2)
            link(v.reciprocal(lb_sum[:, :, :], lb_exp[:, :, :]))
            link(v.tensor_tensor(lb_soft[:, :, :], lb_exp[:, :, :], lb_sum[:, :, :], ALU.mult))
            link(v.tensor_tensor(lb[:, :, :], lb_soft[:, :, :], lb_soft[:, :, :], ALU.subtract))
            link(v.tensor_scalar(lb_floor[:, :, :], lb[:, :, :], LB_FLOOR, None, ALU.max))
            link(v.tensor_scalar(lb_rest[:, :, :], lb[:, :, :], -1.0, 1.0, ALU.mult, ALU.add))
            dve.wait_ge(s_sqm, KT)
            link(v.tensor_scalar(tmp[:, 3, :], ps[:, 2, :], 1.0 / D, RMS_EPS, ALU.mult, ALU.add))
            v.reciprocal(tmp[:, 2, :], tmp[:, 3, :]).then_inc(s_ms, 1)
            dve.wait_ge(s_rs, 1)
            for k in range(KT):
                if k >= 2:
                    dve.wait_ge(s_hl, k - 1)
                v.scalar_tensor_tensor(tmp[:, k % 2, :], xT[:, k, :], cols("norm_w")[:, k:k + 1], tmp[:, 3, :],
                                       ALU.mult, ALU.mult).then_inc(s_h, 1)
            dve.wait_ge(s_setup, 1)
            v.tensor_tensor(cT[:, :, :].rearrange("p k o -> p o k"), c_raw, c_sig[:, :, :],
                            ALU.mult).then_inc(s_setup, 1)

            def flat(x):
                return x[:, :, :].rearrange("p h s -> p (h s)")

            def gla_init(g):
                v.tensor_tensor(qf[:, :, :], q_new[:, :, :], f_f[:, :, :], ALU.mult)
                v.tensor_tensor(qb[:, :, :], q_new[:, :, :], f_b[:, :, :], ALU.mult).then_inc(s_gprep, 1)

            def gla_double(g, l):
                b = 2 ** (l - 1)
                n = 2 * S // (2 * b)
                if l == 1:
                    tots = [flat(f_f), flat(f_b)]
                    dve.wait_ge(s_kcopy, g + 1)
                else:
                    src = tot_a if l % 2 == 0 else tot_b
                    tots = [src[:, d, 0:2 * n] for d in range(2)]
                tf, tb = [x.rearrange("p (n a) -> p n a", a=2) for x in tots]
                dst = tot_a if l % 2 else tot_b
                if l == 1:
                    dve.wait_ge(s_gcp_act, 3 * g + 1)
                dve.wait_ge(s_gla, 12 * g + l + 1)
                if l > 1:
                    dve.wait_ge(s_gcp_dve, 9 * g + l - 1)
                dve.wait_ge(s_gprep, 9 * g + l)
                for x, side, tot in ((qf, 1, tf[:, :, 0]), (kf, 0, tf[:, :, 1]), (qb, 0, tb[:, :, 1]), (kb, 1, tb[:, :, 0])):
                    xv = flat(x).rearrange("p (n a b) -> p n a b", a=2, b=b)[:, :, side, :]
                    last = v.tensor_tensor(xv, xv, tot.unsqueeze(2).to_broadcast([P, n, b]), ALU.mult)
                if l < 8:
                    for d, x in enumerate((tf, tb)):
                        o = v.tensor_tensor(dst[:, d, 0:n], x[:, :, 0], x[:, :, 1], ALU.mult)
                        if d:
                            o.then_inc(s_gprep, 1)
                else:
                    last.then_inc(s_gprep, 1)

            def gla_keep(g, l):
                bank = 2 + 2 * (l % 2)
                v.copy_predicated(a_diag[:, :, :, :].rearrange("p h n s -> p (h n) s"),
                                  masks[:, l - 1, :].unsqueeze(1).to_broadcast([P, 2 * NT, P]),
                                  ps[:, bank:bank + 2, :].rearrange("p a (n s) -> p (a n) s", s=P)).then_inc(s_gcp_dve, 1)

            def gla_norm(g):
                dve.wait_ge(s_gla, 12 * g + 12)
                v.tensor_scalar(kb[:, :, :], ps[:, 4:6, :], 1.0 / P, RMS_EPS, ALU.mult, ALU.add).then_inc(s_gcp_dve, 1)
                dve.wait_ge(s_gcp_dve, 9 * g + 8)
                v.reciprocal(kf[:, :, :], kb[:, :, :]).then_inc(s_gms, 1)
                dve.wait_ge(s_grs, g + 1)
                v.scalar_tensor_tensor(kb[:, :, :], ps[:, 2:4, :], cols("gnorm_w"), qb[:, :, :],
                                       ALU.mult, ALU.mult).then_inc(s_gcp_dve, 1)
                dve.wait_ge(s_gcp_dve, 9 * g + 9)
                v.tensor_tensor(y_a[:, bass.ds(2 * g, 2), :], kb[:, :, :], g_a[:, :, :], ALU.mult).then_inc(s_y, 1)
                dve.wait_ge(s_y, g + 2)

            def head_tiles(it, first):
                g = it - 1
                sig = 12 * it
                for x, s in enumerate(heads.split):
                    kind = HEAD_STRIPS[s]
                    for j in range(2):
                        tt = 2 * x + j
                        if not first:
                            if tt == 0:
                                gla_init(g)
                                dve.wait_ge(s_gla, 12 * g + 1)
                            if tt <= 7:
                                gla_double(g, tt + 1)
                            if 0 <= tt <= 6:
                                gla_keep(g, tt + 1)
                            if tt == 8:
                                dve.wait_ge(s_gla, 12 * g + 11)
                            if tt == 10:
                                gla_norm(g)
                        bank, a, b = ps[:, j, :], tmp[:, 2 * j, :], tmp[:, 2 * j + 1, :]
                        if kind == "q":
                            sig += 1
                            dve.wait_ge(s_sig, sig)
                            v.scalar_tensor_tensor(q_new[:, j, :], bank, float(P) ** -0.5, a,
                                                   ALU.mult, ALU.mult).then_inc(s_free, 1)
                        elif kind == "ga":
                            sig += 1
                            dve.wait_ge(s_sig, sig)
                            v.tensor_tensor(g_a[:, j, :], bank, a, ALU.mult).then_inc(s_free, 1)
                        elif kind == "v":
                            sig += 1
                            dve.wait_ge(s_sig, sig)
                            v.tensor_scalar(b, a, GELU_B, GELU_A, ALU.mult, ALU.add).then_inc(s_dve, 1)
                            link_at(it, 2 * j + 1)
                            v.tensor_tensor(b, b, bank, ALU.mult).then_inc(s_pre, 1)
                            sig += 1
                            dve.wait_ge(s_sig, sig)
                            v.tensor_tensor(vs[:, 2 * j:2 * j + 2, bass.ds(it * STRIP, STRIP)],
                                            bank.rearrange("p (n c) -> p n c", c=STRIP),
                                            a.rearrange("p (n c) -> p n c", c=STRIP), ALU.mult).then_inc(s_free, 1)
                        elif kind == "i":
                            dve.wait_ge(s_proj, heads.t(it, s) + j + 1)
                            v.tensor_copy(v_tok[:, 2 * j:2 * j + 2, :],
                                          bank.rearrange("p (n c) -> p n c", c=STRIP)).then_inc(s_free, 1)
                        else:
                            sig += 1
                            d, f, k = (0, f_f, kf_new) if kind == "ff" else (1, f_b, kb_new)
                            dve.wait_ge(s_sig, sig)
                            col = bass.ds(2 * it + j, 1)
                            v.tensor_scalar(f[:, j, :], a, lb_rest[:, d, col], lb_floor[:, d, col], ALU.mult, ALU.add)
                            v.tensor_scalar(k[:, j, :], b, lb_rest[:, d, col], None, ALU.mult).then_inc(s_free, 1)
                    if kind == "fb":
                        dve.wait_ge(s_free, heads.t(it, s) + 2)
                        v.tensor_tensor(k_sum[:, :, :], kf_new[:, :, :], kb_new[:, :, :], ALU.add).then_inc(s_ks, 1)
                assert isinstance(sig, int) is False or sig == 12 * it + 12, sig
            base = chain["n"]

            def link_at(it, n):
                dve.wait_ge(s_dve, 2 * it + base + (n + 1) // 2)

            head_tiles(0, True)
            with dve.Fori(1, PAIRS) as it:
                head_tiles(it, False)
            chain["n"] = base + 2 * PAIRS

            def gla_slot(g, tt):
                if tt == 0:
                    gla_init(g)
                if tt <= 7:
                    gla_double(g, tt + 1)
                if tt <= 6:
                    gla_keep(g, tt + 1)
                if tt == 10:
                    gla_norm(g)

            def combine(g):
                dve.wait_ge(s_mix, g + 1)
                if g:
                    dve.wait_ge(s_ybl, g)
                link(v.tensor_tensor(tmp[:, 3, :].rearrange("p (n t) -> p n t", t=P), ps[:, 7, :].rearrange("p (n t) -> p n t", t=P),
                                     bs_all[:, g, :].unsqueeze(1).to_broadcast([P, NT, P]), ALU.add))
                dve.wait_ge(s_free, gates.t0 + 2 * g + 2)
                v.tensor_tensor(tmp[:, 3, :], tmp[:, 3, :], u_g[:, :], ALU.mult).then_inc(s_yb, 1)

            def norm_v():
                for n in range(NT):
                    for h in range(2):
                        link(v.bn_stats(v_bn[:, h, :], vs[:, n, h * S:(h + 1) * S]))
                    link(v.bn_aggr(v_stat[:, n, :], v_bn[:, :, :]))
                link(v.tensor_scalar(v_rstd[:, :], v_stat[:, :, 1], LN_EPS, None, ALU.add))
                v.reciprocal(v_stat[:, :, 1], v_rstd[:, :]).then_inc(s_ln, 1)
                dve.wait_ge(s_ln, 2)
                for n in range(NT):
                    v.tensor_scalar(vs[:, n, :], vs[:, n, :], v_stat[:, n, 0:1], v_rstd[:, n:n + 1],
                                    ALU.subtract, ALU.mult).then_inc(s_ln, 1)

            dve.wait_ge(s_lnp, 48)
            dve.wait_ge(s_free, gates.t0)
            for g in range(GCH):
                for j in range(2):
                    tt = 2 * g + j
                    gla_slot(PAIRS - 1, tt)
                    if tt == 0:
                        norm_v()
                    if j == 0:
                        if g:
                            combine(g - 1)
                        dve.wait_ge(s_sigg, 3 * g + 1)
                        link(v.tensor_scalar(tmp[:, 1, :], tmp[:, 0, :], GELU_B, GELU_A, ALU.mult, ALU.add))
                        v.tensor_tensor(tmp[:, 1, :], tmp[:, 1, :], ps[:, 0, :], ALU.mult).then_inc(s_preg, 1)
                        dve.wait_ge(s_sigg, 3 * g + 2)
                        if g:
                            dve.wait_ge(s_yb, g)
                        v.tensor_tensor(u_g[:, :], tmp[:, 0, :], ps[:, 0, :], ALU.mult).then_inc(s_free, 1)
                    else:
                        dve.wait_ge(s_sigg, 3 * g + 3)
                        link(v.tensor_tensor(tmp[:, 2, :], tmp[:, 2, :], ps[:, 1, :], ALU.mult))
                        v.tensor_tensor(u_g[:, :], u_g[:, :], tmp[:, 2, :], ALU.mult).then_inc(s_free, 1)
            combine(GCH - 1)

            base_m = chain["n"]

            def merge_dve(it):
                for x, s in enumerate(merge.split):
                    for j in range(2):
                        col = bass.ds(2 * it + j, 1)
                        if x in (0, 2):
                            dve.wait_ge(s_sigm, 4 * it + x + j + 1)
                            dve.wait_ge(s_free, merge.t(it, s) + j)
                            dve.sem_inc(s_free, 1)
                        elif x == 1:
                            dve.wait_ge(s_proj, merge.t(it, s) + j + 1)
                            v.tensor_tensor(merged[:, col, :], ps[:, j, :], tmp[:, j, :], ALU.mult).then_inc(s_free, 1)
                        else:
                            dve.wait_ge(s_proj, merge.t(it, s) + j + 1)
                            v.tensor_tensor(tmp[:, 2 + j, :], ps[:, j, :], tmp[:, 2 + j, :], ALU.mult).then_inc(s_dve, 1)
                            dve.wait_ge(s_dve, 2 * it + base_m + j + 1)
                            v.tensor_tensor(merged[:, col, :], merged[:, col, :], tmp[:, 2 + j, :], ALU.add).then_inc(s_free, 1)
                dve.wait_ge(s_free, merge.t(it, 4) + 2)
                dve.sem_inc(s_m, 1)
            with dve.Fori(0, merge.iters) as it:
                merge_dve(it)
            chain["n"] = base_m + 2 * merge.iters

            def residual(tiles):
                for k in tiles:
                    dve.wait_ge(s_xe, KT + k + 1)
                    dve.wait_ge(s_proj, outs.t0 + k + 1)
                    v.tensor_tensor(xT[:, k, :], xT[:, k, :], ps[:, k % 2, :], ALU.add).then_inc(s_free, 1)
            residual(range(5))

            cnt = {"n": 0, "h": 0}

            def pair(k):
                return tmp[:, 2 * (k % 2):2 * (k % 2) + 2, :].rearrange("p a s -> p (a s)")

            def norm(n_mm, banks, n, width, eps=RMS_EPS):
                cnt["n"] += 1
                cnt["h"] += n_mm
                dve.wait_ge(s_nmm, cnt["h"])
                o = 0
                for b, w in zip(banks, n):
                    last = v.tensor_scalar(pair(1)[:, o:o + w], ps[:, b, 0:w], 1.0 / width, eps, ALU.mult, ALU.add)
                    o += w
                link(last)
                v.reciprocal(pair(0)[:, 0:o], pair(1)[:, 0:o]).then_inc(s_nms, 1)
                dve.wait_ge(s_nrs, cnt["n"])
                return pair(1)

            def modulation(layer, g):
                a = ada[:, 48 * layer:48 * layer + 48].rearrange("p (m k o) -> p m k o", m=3, o=2)
                b = cols("ada_b_%d_2" % layer).rearrange("p (m k) -> p m k", m=3)
                for o in range(2):
                    last = v.tensor_tensor(a[:, :, :, o], a[:, :, :, o], b, ALU.add)
                link(last)
                link(v.tensor_scalar(mods[:, :, :], a[:, 1, :, :].rearrange("p k o -> p o k"), 1.0, None, ALU.add))
                link(v.tensor_tensor(mods[:, :, :], mods[:, :, :], cols(g).unsqueeze(1).to_broadcast([P, 2, KT]), ALU.mult))
                return a

            dve.wait_ge(s_adaev, 24)
            ada_a = modulation(0, "norm_g_0_2")

            done = {"h": 0}

            def modulate(x, n, a, o, root, rootw):
                for k in range(KT):
                    if k >= 2:
                        dve.wait_ge(s_nhl, done["h"] - 1)
                    link(v.tensor_tensor(tmp[:, k % 2, 0:n], x[:, k, :], root[:, 0:n], ALU.mult))
                    v.tensor_scalar(tmp[:, k % 2, 0:n], tmp[:, k % 2, 0:n], mods[:, o, k:k + 1], a[:, 0, k, o:o + 1],
                                    ALU.mult, ALU.add).then_inc(s_nh, 1)
                    done["h"] += 1

            root = norm(KT, (2,), (C,), D, EPS)
            modulate(xcT, C, ada_a, 1, root, C)
            residual(range(5, KT))
            root = norm(KT, (2,), (S,), D)
            for k in range(KT):
                v.scalar_tensor_tensor(x1T[:, k, :], x1T[:, k, :], cols("final_norm_w")[:, k:k + 1], root[:, 0:S],
                                       ALU.mult, ALU.mult).then_inc(s_nx, 1)
            root = norm(KT, (2,), (S,), D, EPS)
            modulate(x1T, S, ada_a, 0, root, S)

            A_PERM = [(i + 16) % 32 for i in range(32)]
            B_PERM = [(i // 8 ^ 1) * 8 + i % 8 for i in range(32)]

            dve.wait_ge(s_taba, 16 * 3)

            def rope(bank, j, out, perm, cos, sin, r):
                a, b = tmp[:, 2 * j, :], tmp[:, 2 * j + 1, :]
                v.stream_shuffle(a[r, :], bank[r, :], perm)
                link(v.tensor_tensor(b[r, :], bank[r, :], cos[r, :], ALU.mult))
                link(v.tensor_tensor(a[r, :], a[r, :], sin[r, :], ALU.mult))
                return v.tensor_tensor(out, a[r, :], b[r, :], ALU.add)

            ALLP = slice(0, P)
            for it in range(a_q.iters):
                for s in range(2):
                    for j in range(2):
                        m = 4 * it + 2 * s + j
                        dve.wait_ge(s_proj, a_q.t(it, s) + j + 1)
                        link(rope(ps[:, 2 * j, :], j, q_all[:, m, C:ALL], A_PERM, cos_a, sin_a, ALLP))
                        v.tensor_copy(q_all[:, m, 0:C], ps[:, 2 * j + 1, 0:C]).then_inc(s_free, 1)
            for j in range(2):
                dve.wait_ge(s_proj, a_kv.t(0, 0) + j + 1)
                link(rope(ps[:, 2 * j, :], j, tmp[:, 2 * j, :], A_PERM, cos_a, sin_a, ALLP))
                link(v.tensor_copy(tmp[:, 2 * j + 1, 0:C], tmp[:, 2 * j, C:S]))
                link(v.tensor_copy(tmp[:, 2 * j, C:S], tmp[:, 2 * j, 0:C]))
                v.tensor_copy(tmp[:, 2 * j, 0:C], ps[:, 2 * j + 1, 0:C]).then_inc(s_kk, 1)
                dve.wait_ge(s_kk, j + 1)
                dve.sem_inc(s_free, 1)
            for j in range(2):
                dve.wait_ge(s_proj, a_kv.t(0, 1) + j + 1)
                dst = va[:, NC:NC + NT, :] if j == 0 else va[:, 0:NC, :]
                src = ps[:, 2 * j:2 * j + (2, 1)[j], :].rearrange("p a s -> p (a s)").rearrange("p (n c) -> p n c", c=STRIP)
                v.tensor_copy(dst, src).then_inc(s_free, 1)
            dve.wait_ge(s_kd, 2)
            for it in range(a_g.iters):
                for s in range(2):
                    for j in range(2):
                        m = 4 * it + 2 * s + j
                        dve.wait_ge(s_sig2, m + 1)
                        v.tensor_tensor(g_lat[:, m, :], ps[:, 2 * j, :], pair(j)[:, 0:S], ALU.mult)
                        v.tensor_tensor(g_ctx[:, m, :], ps[:, 2 * j + 1, 0:C], pair(j)[:, S:ALL], ALU.mult).then_inc(s_free, 1)

            def peak_a(u, x, i, sink):
                dve.wait_ge(s_sc, u + 1)
                if not (isinstance(u, int) and u < 2):
                    dve.wait_ge(s_tr, u - 1)
                keys, cols_m = a_unit(i)
                n = sum(z - a for a, z in keys)
                src = ps[:, 2 * (x % 2):2 * (x % 2) + 2, :].rearrange("p a s -> p (a s)")[:, 0:n]
                small = a_small[:, x % 2, :]
                (a0, z0), rest = cols_m[0], cols_m[1:]
                if rest and rest[0][0] == z0:
                    cols_m = [(a0, rest[0][1])]
                dst = prob_a[:, x % 2, 0:n]
                return dst, src, small, cols_m, n

            def max_a(u, x, i, h):
                sink, minus = sink_st[:, h:h + 1], sink_st[:, A_GROUP + h:A_GROUP + h + 1]
                dst, src, small, cm, n = peak_a(u, x, i, sink)
                v.tensor_copy(small[:, 7:8], sink)
                if len(cm) == 1:
                    link_s(v.tensor_tensor_reduce(out=dst, in0=src, in1=mask_a[:, 0:n], scale=1.0, scalar=NEG_INF,
                                                  op0=ALU.add, op1=ALU.max, accum_out=small[:, 0:1]))
                else:
                    mk = bass.AP(tensor=mask_a[:, :].tensor, offset=mask_a[:, :].offset,
                                 ap=[mask_a[:, :].ap[0], [C + BLK, 2], [1, C]])
                    link_s(v.tensor_tensor_reduce(out=dst.rearrange("p (a b) -> p a b", a=2), in0=src.rearrange("p (a b) -> p a b", a=2), in1=mk, scale=1.0, scalar=NEG_INF,
                                                  op0=ALU.add, op1=ALU.max, accum_out=small[:, 0:1]))
                v.tensor_scalar(small[:, 1:2], small[:, 0:1], -float(A_HD) ** -0.5, minus, ALU.mult, ALU.min).then_inc(s_neg, 1)

            def link_s(ins):
                own["n"] = own["n"] + 1
                ins.then_inc(s_own, 1)
                dve.wait_ge(s_own, own["n"])
            own = {"n": 0}

            def turned(u, x, n, pT):
                dve.wait_ge(s_tr, u + 1)
                if not (isinstance(u, int) and u < 2):
                    dve.wait_ge(s_pv, u - 1)
                a, w = in_banks(n) * P, n * P
                v.tensor_copy(pT[:, x % 2, a:w], ps[:, 5, 0:w - a]).then_inc(s_cpd, 1)

            def inverse(u, x, sink):
                dve.wait_ge(s_exp, u + 1)
                small = a_small[:, x % 2, :]
                if sink:
                    link_s(v.tensor_tensor(small[:, 4:5], small[:, 2:3], small[:, 3:4], ALU.add))
                    link_s(v.reciprocal(small[:, 5:6], small[:, 4:5]))
                else:
                    link_s(v.reciprocal(small[:, 5:6], small[:, 2:3]))

            def weighed(u, x, dst):
                dve.wait_ge(s_pv, u + 1)
                v.tensor_scalar(dst, ps[:, 6, 0:A_HD], a_small[:, x % 2, 6:7], None, ALU.mult).then_inc(s_oo, 1)

            def a_group(g, xs, first=False):
                own["n"] = 0 if first else 4 * A_UNITS * g - 3 + (xs[0] > 0) * 4 * A_UNITS
                for x in xs:
                    if x == 0:
                        if not first:
                            dve.wait_ge(s_exp, A_UNITS * g)
                        heads_g = sink8[:, bass.ds(A_GROUP * g, A_GROUP)]
                        v.tensor_copy(sink_st[:, 0:A_GROUP], heads_g)
                        v.tensor_scalar(sink_st[:, A_GROUP:2 * A_GROUP], heads_g, -1.0, None, ALU.mult)
                        v.tensor_copy(q_st[:, :, :], q_all[:, bass.ds(2 * g, 2), :])
                        v.tensor_copy(k_st[:, :], k_all[:, bass.ds(g, 1), :]).then_inc(s_stage, 1)
                        dve.wait_ge(s_stage, g + 1)
                    if x < A_UNITS:
                        u, _, y, i, h = a_step(g, x)
                        max_a(u, y, i, h)
                    if not (first and x < 1) and x <= A_UNITS:
                        u, _, y, i, _ = a_step(g, x - 1)
                        turned(u, y, len(blocks_of(a_unit(i)[0])), probT_a)
                    if not (first and x < 2):
                        u, gx, y, i, h = a_step(g, x - 2)
                        weighed(u, y, o_tok[:, i, bass.ds(A_GROUP * A_HD * gx + A_HD * h, A_HD)])
                    if not (first and x < 1) and x <= A_UNITS:
                        u, _, y, _, _ = a_step(g, x - 1)
                        inverse(u, y, True)
                        keep = a_small[:, y % 2, :]
                        link_s(v.tensor_copy(keep[:, 6:7], keep[:, 5:6]))
            dve.wait_ge(s_mska, 16)
            dve.wait_ge(s_free, a_out.t0)
            a_group(0, range(A_UNITS), True)
            with dve.Fori(1, A_KV) as g:
                a_group(g, range(A_UNITS))
            a_group(A_KV - 1, (A_UNITS, A_UNITS + 1))
            own["n"] = 4 * A_UNITS * A_KV

            def gated(c0, ctx_):
                for k in range(KT):
                    dve.wait_ge(s_ot, c0 + k + 1)
                    if k >= 2:
                        dve.wait_ge(s_nhl, done["h"] - 1)
                    last = v.tensor_tensor(pair(k)[:, 0:S], ps[:, 2 * (k % 2), :], g_lat[:, k, :], ALU.mult)
                    if ctx_:
                        link(last)
                        last = v.tensor_tensor(pair(k)[:, S:ALL], ps[:, 2 * (k % 2) + 1, 0:C], g_ctx[:, k, :], ALU.mult)
                    last.then_inc(s_nh, 1)
                    done["h"] += 1
                    dve.wait_ge(s_nh, done["h"])
                    dve.sem_inc(s_og, 1)
            gated(0, True)
            for k in range(KT):
                j = k % 2
                dve.wait_ge(s_proj, a_out.t0 + k + 1)
                v.scalar_tensor_tensor(x1T[:, k, :], ps[:, 2 * j, :], ada_a[:, 2, k, 0:1], x1T[:, k, :], ALU.mult, ALU.add)
                v.scalar_tensor_tensor(xcT[:, k, :], ps[:, 2 * j + 1, 0:C], ada_a[:, 2, k, 1:2], xcT[:, k, :],
                                       ALU.mult, ALU.add).then_inc(s_free, 1)
            ada_b = modulation(1, "norm_g_1_2")
            root = norm(KT, (2,), (S,), D, EPS)
            modulate(x1T, S, ada_b, 0, root, S)
            root = norm(KT, (2,), (C,), D, EPS)
            modulate(xcT, C, ada_b, 1, root, C)
            for j in range(2):
                dve.wait_ge(s_proj, b_in.t0 + j + 1)
                v.tensor_copy(cq[:, j, :], ps[:, j, :]).then_inc(s_free, 1)
            root = norm(2, (4,), (S,), B_QR, EPS)
            for k in range(2):
                v.scalar_tensor_tensor(tmp[:, k, :], cq[:, k, :], cols("b_q_norm_1_2")[:, k:k + 1], root[:, 0:S],
                                       ALU.mult, ALU.mult).then_inc(s_nh, 1)
                done["h"] += 1
            dve.wait_ge(s_proj, b_in.t0 + 3)
            v.tensor_copy(ckv[:, C:ALL], ps[:, 0, :])
            v.tensor_copy(ckv[:, 0:C], ps[:, 1, 0:C]).then_inc(s_free, 1)
            dve.wait_ge(s_proj, b_in.t0 + 4)
            v.tensor_copy(kr[3 * 32:P, C:ALL], ps[3 * 32:P, 2, :])
            v.tensor_copy(kr[3 * 32:P, 0:C], ps[3 * 32:P, 3, 0:C]).then_inc(s_free, 1)
            root = norm(1, (6, 7), (S, C), B_KVR, EPS)
            v.scalar_tensor_tensor(pair(0)[:, 0:S], ckv[:, 0:S], cols("b_kv_norm_1_2")[:, 0:1], root[:, 0:S], ALU.mult, ALU.mult)
            v.scalar_tensor_tensor(pair(0)[:, S:ALL], ckv[:, S:ALL], cols("b_kv_norm_1_2")[:, 0:1], root[:, S:ALL],
                                   ALU.mult, ALU.mult).then_inc(s_nh, 1)
            done["h"] += 1
            for it in range(b_g.iters):
                for s in range(2):
                    for j in range(2):
                        m = 4 * it + 2 * s + j
                        dve.wait_ge(s_sig2, KT + m + 1)
                        v.tensor_tensor(g_lat[:, m, :], ps[:, j, :], pair(j)[:, 0:S], ALU.mult).then_inc(s_free, 1)
            dve.wait_ge(s_tabb, 32)
            R = slice(B_NOPE, B_QK)
            K96 = slice(3 * 32, P)
            dve.wait_ge(s_free, b_v.t0)
            link(v.tensor_copy(k_b[R, 0, :], kr[K96, :]))
            link(rope(k_b[:, 0, C:ALL], 0, k_b[R, 0, C:ALL], B_PERM, cos_b, sin_b, R))
            link(v.tensor_copy(k_b[R, 1, :], k_b[R, 0, :]))
            nv = 0
            for s in range(2):
                for i in range(NC + NT):
                    dve.wait_ge(s_vp, nv + 1)
                    v.tensor_copy(vb[:, i, s * S:(s + 1) * S], ps[:, nv % 2, :]).then_inc(s_vb, 1)
                    nv += 1

            def up(h, part):
                b = h % 2
                dve.wait_ge(s_up, 3 * h + part + 1)
                if part == 0:
                    QR = slice(0, B_QK)
                    v.stream_shuffle(tmp[R, 2, :], ps[R, 7, :], B_PERM)
                    link(v.tensor_tensor(q_b[QR, b, :], ps[QR, 7, :], cos_b[QR, :], ALU.mult))
                    link(v.tensor_tensor(tmp[R, 2, :], tmp[R, 2, :], sin_b[R, :], ALU.mult))
                    last = v.tensor_tensor(q_b[R, b, :], q_b[R, b, :], tmp[R, 2, :], ALU.add)
                elif part == 1:
                    last = v.tensor_copy(k_b[0:B_NOPE, b, C:ALL], ps[0:B_NOPE, 7, :])
                else:
                    last = v.tensor_copy(k_b[0:B_NOPE, b, 0:C], ps[0:B_NOPE, 7, 0:C])
                last.then_inc(s_upe, 1)

            for part in range(3):
                up(0, part)
            units = [(h, i) for h in range(B_HEADS) for i in range(NT)]
            A_ALL = A_KV * A_UNITS
            for x in range(len(units) + 2):
                u = A_ALL + x
                if x < len(units):
                    dve.wait_ge(s_sc, u + 1)
                    src = ps[:, 2 * (x % 2):2 * (x % 2) + 2, :].rearrange("p a s -> p (a s)")[:, 0:ALL]
                    link_s(v.reduce_max(a_small[:, x % 2, 0:1], src, AX.X))
                    v.tensor_scalar(a_small[:, x % 2, 1:2], a_small[:, x % 2, 0:1], -float(B_QK) ** -0.5, None,
                                    ALU.mult).then_inc(s_neg, 1)
                if 1 <= x <= len(units):
                    turned(u - 1, x - 1, NC + NT, probT_b)
                if x >= 2:
                    h, i = units[x - 2]
                    weighed(u - 2, x - 2, o_b[:, i, h * B_V:(h + 1) * B_V])
                if 1 <= x <= len(units):
                    inverse(u - 1, x - 1, False)
                    keep = a_small[:, (x - 1) % 2, :]
                    link_s(v.tensor_copy(keep[:, 6:7], keep[:, 5:6]))
                if x < len(units):
                    h, i = units[x]
                    if i < 3 and h + 1 < B_HEADS:
                        up(h + 1, i)
            gated(KT, False)
            for k in range(KT):
                dve.wait_ge(s_proj, b_out.t0 + k + 1)
                v.scalar_tensor_tensor(x1T[:, k, :], ps[:, k % 2, :], ada_b[:, 2, k, 0:1], x1T[:, k, :],
                                       ALU.mult, ALU.add).then_inc(s_free, 1)
            root = norm(KT, (2,), (S,), D, EPS)
            for k in range(KT):
                v.scalar_tensor_tensor(x1T[:, k, :], x1T[:, k, :], cols("final_g_2")[:, k:k + 1], root[:, 0:S],
                                       ALU.mult, ALU.mult).then_inc(s_nx, 1)

        @block.tensor
        def _(pe):
            mm = nc.tensor.matmul
            pe.wait_ge(s_x, 16)
            pe.wait_ge(s_const, N_CONST)
            pe.wait_ge(s_ones, 1)
            nc.tensor.transpose(ps[:, 3, 0:VROWS], vec_rows[0:VROWS, :], ident[0:VROWS, 0:VROWS]).then_inc(s_vt, 1)
            for k in range(KT):
                if k >= 2:
                    pe.wait_ge(s_xe, k - 1)
                for n in range(NT):
                    last = nc.tensor.transpose(ps[:, k % 2, n * P:(n + 1) * P], x_tok[:, n, k * P:(k + 1) * P], ident[:, :])
                last.then_inc(s_xt, 1)
                if k:
                    pe.wait_ge(s_sq, k)
                    mm(ps[:, 2, :], ones[:, :], tmp[:, (k - 1) % 2, :], start=(k == 1), stop=False).then_inc(s_sqm, 1)
            pe.wait_ge(s_sq, KT)
            mm(ps[:, 2, :], ones[:, :], tmp[:, (KT - 1) % 2, :], start=False, stop=True).then_inc(s_sqm, 1)
            pe.wait_ge(s_ws, 16)
            for g in range(GCH):
                last = nc.tensor.transpose(ps[:, 4 + g // 4, g % 4 * P:(g % 4 + 1) * P], wsT[:, g, :], ident[:, :])
            last.then_inc(s_wst, 1)

            def project(ph, it, s, j, tok, xh=h_hi, xl=h_lo, ready=None):
                pe.wait_ge(s_lo, ph.k(it, s) + 1)
                t0 = ph.t(it, s) + j
                if not (isinstance(t0, int) and t0 < 2):
                    pe.wait_ge(s_free, t0 - 1)
                wh, wl = k_of(w_hi, ph.w(s)), k_of(w_lo, ph.w(s))
                if tok:
                    for n in range(2):
                        tk = slice((2 * j + n) * P, (2 * j + n + 1) * P)
                        out = ps[:, j, n * STRIP:(n + 1) * STRIP]
                        for k in range(KT):
                            mm(out, h_hi[:, k, tk], wh[:, k, :], start=(k == 0), stop=False)
                            mm(out, h_hi[:, k, tk], wl[:, k, :], start=False, stop=False)
                            last = mm(out, h_lo[:, k, tk], wh[:, k, :], start=False, stop=(k == KT - 1))
                else:
                    c = slice(j * P, (j + 1) * P)
                    for k in range(KT):
                        if ready:
                            pe.wait_ge(ready[0], ready[1] + k + 1)
                        mm(ps[:, j, :], wh[:, k, c], xh[:, k, :], start=(k == 0), stop=False)
                        mm(ps[:, j, :], wh[:, k, c], xl[:, k, :], start=False, stop=False)
                        last = mm(ps[:, j, :], wl[:, k, c], xh[:, k, :], start=False, stop=(k == KT - 1))
                last.then_inc(s_proj, 1)

            def ada_strip(ph, it, s, bank=None):
                a = ph.a(it, s)
                pe.wait_ge(s_raw[s % 2], 16 * ph.n(it, s) + 32 - 16 * (s % 2))
                if bank == 6:
                    pe.wait_ge(s_adaev, a)
                elif not (isinstance(a, int) and a < 2):
                    pe.wait_ge(s_adaev, a - 1)
                bank = 6 + ph.j(s) if bank is None else bank
                w = k_of(raw, s % 2)
                for m in range(2):
                    for k in range(KT):
                        last = mm(ps[:, bank, 2 * m:2 * m + 2], w[:, k, m * P:(m + 1) * P], cT[:, k, :],
                                  start=(k == 0), stop=(k == KT - 1))
                last.then_inc(s_ada, 1)

            def gla(g, step):
                if step == 0:
                    pe.wait_ge(s_ks, g + 1)
                    pe.wait_ge(s_y, g + 1)
                    for h in range(2):
                        for n in range(NT):
                            tk = slice(n * P, (n + 1) * P)
                            last = mm(ps[:, 2 + h, tk], k_sum[:, h, tk], q_new[:, h, tk], start=True, stop=True)
                elif step <= 7:
                    b = 2 ** (step - 1)
                    pe.wait_ge(s_gprep, 9 * g + step)
                    if step == 1:
                        pe.wait_ge(s_kcopy, g + 1)
                    elif step == 2:
                        pe.wait_ge(s_gcp_act, 3 * g + 1)
                    else:
                        pe.wait_ge(s_gcp_dve, 9 * g + step - 2)
                    for h in range(2):
                        for n in range(NT):
                            tk = slice(n * P, (n + 1) * P)
                            o = ps[:, 2 + 2 * (step % 2) + h, tk].rearrange("p (m a b) -> p m a b", a=2, b=b)
                            for side, q, k in ((1, qf, kf), (0, qb, kb)):
                                qv = q[:, h, tk].rearrange("p (m a b) -> p m a b", a=2, b=b)[:, :, side, :]
                                last = mm(o[:, :, side, :], k[:, h, tk], qv, start=True, stop=True)
                elif step == 8:
                    pe.wait_ge(s_gprep, 9 * g + 8)
                    pe.wait_ge(s_gcp_dve, 9 * g + 6)
                    for h in range(2):
                        for n in range(NT):
                            q, k = (qb, kb) if n % 2 else (qf, kf)
                            m = n ^ 1
                            last = mm(ps[:, 2 + h, n * P:(n + 1) * P], k[:, h, n * P:(n + 1) * P],
                                      q[:, h, m * P:(m + 1) * P], start=True, stop=True)
                elif step == 9:
                    pe.wait_ge(s_gprep, 9 * g + 9)
                    pe.wait_ge(s_gcp_dve, 9 * g + 7)
                    pe.wait_ge(s_gcp_act, 3 * g + 2)
                    for h in range(2):
                        for n in range(NT):
                            q, k, c = (qf, kf, S // 2) if n < 2 else (qb, kb, 0)
                            last = mm(ps[:, 2 + 2 * h + n // 2, (n % 2) * 2 * P:(n % 2 + 1) * 2 * P],
                                      k[:, h, n * P:(n + 1) * P], q[:, h, c:c + S // 2], start=True, stop=True)
                elif step == 10:
                    pe.wait_ge(s_gcp_act, 3 * g + 3)
                    for h in range(2):
                        for n in range(NT):
                            out = ps[:, 2 + h, n * P:(n + 1) * P]
                            far = [2, 3] if n < 2 else [0, 1]
                            att = [(n, a_diag[:, h, n, :]), (n ^ 1, a_128[:, h, n ^ 1, :])]
                            att += [(m, a_256[:, h, m, (n % 2) * P:(n % 2 + 1) * P]) for m in far]
                            for i, (m, a) in enumerate(att):
                                last = mm(out, v_tok[:, m, h * P:(h + 1) * P], a, start=(i == 0), stop=(i == 3))
                else:
                    pe.wait_ge(s_osq, g + 1)
                    for h in range(2):
                        last = mm(ps[:, 4 + h, :], ones[:, :], qf[:, h, :], start=True, stop=True)
                last.then_inc(s_gla, 1)

            def head_tiles(it, first):
                for s, kind in enumerate(HEAD_STRIPS):
                    if kind == "ada":
                        if first and s == 3:
                            pe.wait_ge(s_setup, 2)
                        ada_strip(heads, it, s)
                        continue
                    for j in range(2):
                        tt = 2 * heads.split.index(s) + j
                        project(heads, it, s, j, kind in ("v", "i"), ready=(s_hl, 0) if first and tt == 0 else None)
                        if not first:
                            if tt == 0:
                                gla(it - 1, 0)
                            if tt <= 10:
                                gla(it - 1, tt + 1)
            head_tiles(0, True)
            with pe.Fori(1, PAIRS) as it:
                head_tiles(it, False)

            def mix(g):
                if g == 0:
                    pe.wait_ge(s_vs, NT)
                    pe.wait_ge(s_wst, 2)
                    pe.wait_ge(s_adaev, gates.a0)
                else:
                    pe.wait_ge(s_yb, g)
                for n in range(NT):
                    last = mm(ps[:, 7, n * P:(n + 1) * P], vs[:, n, g * P:(g + 1) * P], wsT[:, g, :], start=True, stop=True)
                last.then_inc(s_mix, 1)

            for g in range(GCH):
                it, s = g // 2, 2 * (g % 2)
                for j in range(2):
                    tt = 2 * g + j
                    if tt == 0:
                        gla(PAIRS - 1, 0)
                    if tt <= 10:
                        gla(PAIRS - 1, tt + 1)
                    project(gates, it, s, j, False)
                    if j == 0 and g:
                        mix(g - 1)
                ada_strip(gates, it, s + 1, 6)
            mix(GCH - 1)
            pe.wait_ge(s_yal, KT)
            pe.wait_ge(s_ybl, GCH)
            with pe.Fori(0, merge.iters) as it:
                for s, kind in enumerate(MERGE_STRIPS):
                    if kind == "ada":
                        ada_strip(merge, it, s, 7 - merge.j(s))
                        continue
                    for j in range(2):
                        x_hi, x_lo = {"pa": (ya_hi, ya_lo), "pb": (yb_hi, yb_lo)}.get(kind, (h_hi, h_lo))
                        project(merge, it, s, j, False, x_hi, x_lo)
            pe.wait_ge(s_x2, 16)
            for k in range(KT):
                if k >= 4:
                    pe.wait_ge(s_xe, KT + k - 3)
                for n in range(NT):
                    last = nc.tensor.transpose(ps[:, 2 + k % 4, n * P:(n + 1) * P], x_again[:, n, k * P:(k + 1) * P], ident[:, :])
                last.then_inc(s_xt, 1)
            pe.wait_ge(s_ml, KT)

            cnt = {"sq": 0, "mm": 0, "nh": 0, "nx": 0}

            def norm(src_tiles, n, banks=(2,)):
                for k in range(src_tiles):
                    cnt["sq"] += 1
                    pe.wait_ge(s_nsq, cnt["sq"])
                    for b, w in zip(banks, n):
                        src = (tmp[:, k % 2, :] if len(banks) == 1 else
                               tmp[:, 2 * (k % 2):2 * (k % 2) + 2, :].rearrange("p a s -> p (a s)"))
                        o = 0 if b == banks[0] else n[0]
                        last = mm(ps[:, b, 0:w], ones[:, :], src[:, o:o + w], start=(k == 0), stop=(k == src_tiles - 1))
                    last.then_inc(s_nmm, 1)

            def out_tile(m):
                project(outs, m // 4, m // 2 % 2, m % 2, False)

            for m in range(2):
                out_tile(m)
            pe.wait_ge(s_in2, 16)
            pe.wait_ge(s_adaev, 24)
            pe.wait_ge(s_xe, 2 * KT)
            for k in range(KT):
                if k >= 2:
                    pe.wait_ge(s_ctx, k - 1)
                for n in range(NC):
                    last = nc.tensor.transpose(ps[:, 6 + k % 2, n * P:(n + 1) * P], c_tok[:, n, k * P:(k + 1) * P], ident[:, :])
                last.then_inc(s_ct, 1)
            for m in range(2, 5):
                out_tile(m)
            norm(KT, [C])
            for m in range(5, KT):
                out_tile(m)
            norm(KT, [S])
            norm(KT, [S])

            def project2(ph, it, s, j, lat, ctx_, c, kt=KT, k_n=STRIP, ready=None):
                pe.wait_ge(s_lo, ph.k(it, s) + 1)
                pe.wait_ge(s_free, ph.t(it, s) + j - 1)
                wh, wl = k_of(w_hi, s % 2, k_n), k_of(w_lo, s % 2, k_n)
                for k in range(kt):
                    if ready:
                        pe.wait_ge(ready[0], ready[1] + k + 1)
                    for o, (xh, xl) in ((ps[:, 2 * j, :], lat), (ps[:, 2 * j + 1, 0:C], ctx_)):
                        mm(o, wh[:, k, c], xh[:, k, :], start=(k == 0), stop=False)
                        mm(o, wh[:, k, c], xl[:, k, :], start=False, stop=False)
                        last = mm(o, wl[:, k, c], xh[:, k, :], start=False, stop=(k == kt - 1))
                last.then_inc(s_proj, 1)

            H, HC = (h_hi, h_lo), (hc_hi, hc_lo)

            def both(ph, ready=None):
                for it in range(ph.iters):
                    for s in range(2):
                        for j in range(2):
                            project2(ph, it, s, j, H, HC, slice(j * P, (j + 1) * P), ready=None if it or s or j else ready)
            both(a_q, (s_nhl, KT))
            for j in range(2):
                project2(a_kv, 0, 0, j, H, HC, slice(j * P, (j + 1) * P))
            for j in range(2):
                pe.wait_ge(s_lo, a_kv.k(0, 1) + 1)
                pe.wait_ge(s_free, a_kv.t(0, 1) + j - 1)
                wh, wl = k_of(w_hi, 1), k_of(w_lo, 1)
                for n in range((NT, NC)[j]):
                    xh, xl = (H, HC)[j]
                    out = ps[:, 2 * j + n // 2, n % 2 * STRIP:(n % 2 + 1) * STRIP]
                    tk = slice(n * P, (n + 1) * P)
                    for k in range(KT):
                        mm(out, xh[:, k, tk], wh[:, k, :], start=(k == 0), stop=False)
                        mm(out, xh[:, k, tk], wl[:, k, :], start=False, stop=False)
                        last = mm(out, xl[:, k, tk], wh[:, k, :], start=False, stop=(k == KT - 1))
                last.then_inc(s_proj, 1)
            both(a_g)
            pe.wait_ge(s_free, a_out.t0)

            def scores(u, parts):
                if not (isinstance(u, int) and u < 2):
                    pe.wait_ge(s_exp, u - 1)
                for col, q, k in parts:
                    n = k.shape[-1]
                    b = 2 * par(u) + col // S
                    last = mm(ps[:, b, col % S:col % S + n], q, k, start=True, stop=True)
                last.then_inc(s_sc, 1)

            par_of = [0]

            def par(u):
                return par_of[0] % 2

            def turn(u, p, n, prob):
                pe.wait_ge(s_exp, u + 1)
                if not (isinstance(u, int) and u < 1):
                    pe.wait_ge(s_cpa, u)
                    pe.wait_ge(s_cpd, u)
                a = in_banks(n)
                for b in range(n):
                    o = ps[:, 4, b * P:(b + 1) * P] if b < a else ps[:, 5, (b - a) * P:(b - a + 1) * P]
                    last = nc.tensor.transpose(o, prob[:, p, b * P:(b + 1) * P], ident[:, :])
                last.then_inc(s_tr, 1)

            def weigh(u, p, blocks, pT, val):
                pe.wait_ge(s_cpa, u + 1)
                pe.wait_ge(s_cpd, u + 1)
                if not (isinstance(u, int) and u < 1):
                    pe.wait_ge(s_oo, u)
                for i, b in enumerate(blocks):
                    last = mm(ps[:, 6, 0:A_HD], pT[:, p, i * P:(i + 1) * P], val(b), start=(i == 0), stop=(i == len(blocks) - 1))
                last.then_inc(s_pv, 1)

            def keep_busy(n, width=S):
                for _ in range(n):
                    mm(ps[:, 7, 0:width], q_all[:, 0, 0:P], q_all[:, 1, 0:width], start=True, stop=True)

            def a_scores(g, x):
                u, _, y, i, h = a_step(g, x)
                r = slice(h % 2 * A_HD, (h % 2 + 1) * A_HD)
                par_of[0] = y
                if x == 0:
                    pe.wait_ge(s_stage, g + 1)
                scores(u, [(col, q_st[r, h // 2, i * P:(i + 1) * P], k_st[r, k0:k0 + n])
                           for col, k0, n in score_parts(a_unit(i)[0])])

            def a_group(g, xs, first=False):
                for x in xs:
                    if 0 < x < A_UNITS:
                        a_scores(g, x)
                    if first and x < 2:
                        keep_busy(BUSY[x])
                    elif x < A_UNITS:
                        keep_busy(1, C)
                    if not (first and x < 2):
                        u, gx, y, i, h = a_step(g, x - 2)
                        weigh(u, y % 2, blocks_of(a_unit(i)[0]), probT_a, lambda b: va[:, b, bass.ds(A_HD * gx, A_HD)])
                    if not (first and x < 1) and x <= A_UNITS:
                        u, _, y, i, _ = a_step(g, x - 1)
                        turn(u, y % 2, len(blocks_of(a_unit(i)[0])), prob_a)
                    if x == 0:
                        a_scores(g, x)
            pe.wait_ge(s_kd, 2)
            a_group(0, range(A_UNITS), True)
            with pe.Fori(1, A_KV) as g:
                a_group(g, range(A_UNITS))
            a_group(A_KV - 1, (A_UNITS, A_UNITS + 1))

            def gated(first, tiles, src, c0):
                pe.wait_ge(s_oo, first)
                for k in range(KT):
                    if k >= 2:
                        pe.wait_ge(s_og, c0 + k - 1)
                    for i in range(tiles):
                        lat = i >= tiles - NT
                        n = i - (tiles - NT) if lat else i
                        last = nc.tensor.transpose(ps[:, 2 * (k % 2) + (0 if lat else 1), n * P:(n + 1) * P],
                                                   src[:, i, k * P:(k + 1) * P], ident[:, :])
                    last.then_inc(s_ot, 1)
            A_ALL = A_KV * A_UNITS
            gated(A_ALL, NC + NT, o_tok, 0)
            pe.wait_ge(s_nhl, 3 * KT)
            pe.wait_ge(s_og, KT)
            for it in range(2):
                for s in range(2):
                    for j in range(2):
                        project2(a_out, it, s, j, (ya_hi, ya_lo), (yc_hi, yc_lo), slice(j * P, (j + 1) * P))
            pe.wait_ge(s_free, b_in.t0)
            norm(KT, [S])
            project(b_in, 0, 0, 0, False, ready=(s_nhl, 3 * KT))
            norm(KT, [C])
            project(b_in, 0, 0, 1, False)
            pe.wait_ge(s_nhl, 5 * KT)
            pe.wait_ge(s_free, b_in.t0 + 2)
            for j in range(2):
                project2(b_in, 0, 1, j, H, HC, slice(j * B_ROPE, j * B_ROPE + P), k_n=B_KVR + B_ROPE)
                if j == 0:
                    norm(2, [S], (4,))
            for it in range(2):
                for s in range(2):
                    for j in range(2):
                        project(b_g, it, s, j, False)
                        if it == s == j == 0:
                            norm(1, [S, C], (6, 7))
            pe.wait_ge(s_nhl, 5 * KT + 3)
            def v_cols(w, s):
                return w[:, s, 0:D].rearrange("p (h a c) -> p h a c", a=2, c=B_V)[:, :, 1, :]
            nv = 0
            for s in range(2):
                pe.wait_ge(s_lo, b_v.k(0, s) + 1)
                for i in range(NC + NT):
                    if nv >= 2:
                        pe.wait_ge(s_vb, nv - 1)
                    else:
                        pe.wait_ge(s_free, b_v.t0)
                    out = ps[:, nv % 2, :].rearrange("p (h c) -> p h c", c=B_V)
                    tk = slice(i * P, (i + 1) * P)
                    mm(out, ckv_hi[:, tk], v_cols(w_hi, s), start=True, stop=False)
                    mm(out, ckv_hi[:, tk], v_cols(w_lo, s), start=False, stop=False)
                    last = mm(out, ckv_lo[:, tk], v_cols(w_hi, s), start=False, stop=True)
                    nv += 1
                    last.then_inc(s_vp, 1)
            pe.wait_ge(s_vb, 2 * (NC + NT))

            def up(h, part, u):
                s, j = h // 2 % 2, h % 2
                if part == 0:
                    pe.wait_ge(s_lo, b_up.k0 + h // 2 + 1)
                if 3 * h + part:
                    pe.wait_ge(s_upe, 3 * h + part)
                if part == 0:
                    for k in range(2):
                        c = slice(2 * B_QK * k + j * B_QK, 2 * B_QK * k + (j + 1) * B_QK)
                        o = ps[0:B_QK, 7, :]
                        mm(o, w_hi[:, s, c], cq_hi[:, k, :], start=(k == 0), stop=False)
                        mm(o, w_hi[:, s, c], cq_lo[:, k, :], start=False, stop=False)
                        last = mm(o, w_lo[:, s, c], cq_hi[:, k, :], start=False, stop=(k == 1))
                else:
                    c = slice(4 * B_QK + j * P, 4 * B_QK + (j + 1) * P)
                    tk = slice(C, ALL) if part == 1 else slice(0, C)
                    o = ps[:, 7, 0:S if part == 1 else C]
                    mm(o, w_hi[:, s, c], ckv_hi[:, tk], start=True, stop=False)
                    mm(o, w_hi[:, s, c], ckv_lo[:, tk], start=False, stop=False)
                    last = mm(o, w_lo[:, s, c], ckv_hi[:, tk], start=False, stop=True)
                last.then_inc(s_up, 1)

            for part in range(3):
                up(0, part, 0)
            units = [(h, i) for h in range(B_HEADS) for i in range(NT)]
            for x in range(len(units) + 2):
                if x < len(units):
                    h, i = units[x]
                    if i == 0:
                        pe.wait_ge(s_upe, 3 * h + 3)
                    par_of[0] = x
                    scores(A_ALL + x, [(col, q_b[0:B_QK, h % 2, i * P:(i + 1) * P], k_b[0:B_QK, h % 2, k0:k0 + n])
                                       for col, k0, n in score_parts([(0, ALL)])])
                if x >= 2:
                    h, i = units[x - 2]
                    weigh(A_ALL + x - 2, x % 2, list(range(NC + NT)), probT_b, lambda b: vb[:, b, h * B_V:(h + 1) * B_V])
                if 1 <= x <= len(units):
                    turn(A_ALL + x - 1, (x - 1) % 2, NC + NT, prob_b)
                if x < len(units):
                    h, i = units[x]
                    if i < 3 and h + 1 < B_HEADS:
                        up(h + 1, i, x)
            B_ALL = A_ALL + B_HEADS * NT
            gated(B_ALL, NT, o_b, KT)
            pe.wait_ge(s_nhl, 6 * KT + 3)
            pe.wait_ge(s_og, 2 * KT)
            for it in range(2):
                for s in range(2):
                    for j in range(2):
                        project(b_out, it, s, j, False, ya_hi, ya_lo)
            norm(KT, [S])
            for n in range(NT):
                for h in range(2):
                    x = 2 * n + h
                    pe.wait_ge(s_nx, KT + KT)
                    if x >= 2:
                        pe.wait_ge(s_fe, x - 1)
                    for i in range(4):
                        k = 4 * h + i
                        last = nc.tensor.transpose(ps[:, 4 + x % 2, i * P:(i + 1) * P], x1T[:, k, n * P:(n + 1) * P], ident[:, :])
                    last.then_inc(s_ft, 1)


NSPLIT_H = sum(s != "ada" for s in HEAD_STRIPS)


def tables():
    import numpy as np
    i = np.arange(P)
    masks = np.zeros((7, P, P), np.float32)
    for l in range(7):
        b = 2 ** l
        masks[l] = (i[:, None] // (2 * b) == i[None, :] // (2 * b)) & (i[:, None] // b != i[None, :] // b)
    row, col = np.arange(S) // 64, np.arange(S) % 64

    def rotary(dim, heads, ahead=0):
        nf = dim // 4
        inv = np.float32(10000.0) ** (-np.arange(nf, dtype=np.float32) / np.float32(nf))
        ar, ac = row.astype(np.float32)[:, None] * inv, col.astype(np.float32)[:, None] * inv
        ang = np.concatenate([ar, ar, ac, ac], axis=-1)
        sign = np.repeat(np.array([-1, 1, -1, 1], np.float32), nf)
        cos = np.concatenate([np.ones((ahead, S), np.float32), np.cos(ang).T])
        sin = np.concatenate([np.zeros((ahead, S), np.float32), np.sin(ang).T * sign[:, None]])
        return np.tile(cos, (heads, 1)).astype(np.float32), np.tile(sin, (heads, 1)).astype(np.float32)

    cos_a, sin_a = rotary(A_HD, 2)
    cos_b, sin_b = rotary(B_ROPE, 1, B_NOPE)
    mask_a = np.zeros((P, C + 3 * BLK), np.float32)
    mask_a[:, C:C + BLK][i[None, :] < i[:, None]] = NEG_INF
    mask_a[:, C + 2 * BLK:][i[None, :] > i[:, None]] = NEG_INF
    return {"ident": np.eye(P, dtype=np.float32), "masks": masks, "cos_a": cos_a, "sin_a": sin_a,
            "cos_b": cos_b, "sin_b": sin_b, "mask_a": mask_a}


OUT_SHAPE = (1, S, D)


def kernel(**inputs):
    import numpy as _np
    import concourse.bacc as _bacc
    from concourse import mybir as _mybir
    from concourse.bass_utils import run_bass_kernel_spmd as _run

    nc = _bacc.Bacc("TRN2", target_bir_lowering=False, num_devices=1)
    arrays, t = {}, {}
    for name, value in list(inputs.items()) + list(tables().items()):
        a = _np.ascontiguousarray(value)
        arrays[f"in_{name}_dram"] = a
        t[name] = nc.dram_tensor(f"in_{name}_dram", a.shape, _mybir.dt.from_np(a.dtype), kind="ExternalInput").ap()
    t["out"] = nc.dram_tensor("out_0_dram", OUT_SHAPE, _mybir.dt.float32, kind="ExternalOutput").ap()
    block_kernel(nc, t)
    r = _run(nc, [arrays], core_ids=[0])
    return r.results[0]["out_0_dram"]
```
